# Optimizing a Trainium2 kernel written in Bass

```python
import math
import jax
import jax.numpy as jnp
from jax import lax
import numpy as np

D_MODEL = 1024
BATCH = 1
SEQ = 512
DEPTH = 1

ATTN_HEADS = 8
HEAD_DIM = 64
ATTN_WIDTH = ATTN_HEADS * HEAD_DIM
MOBA_BLOCK = 256
MOBA_TOPK = 3
MOBA_QCHUNK = 128
REL_BUCKETS = 32
REL_MAX_DISTANCE = 2048
GMLP_WIDTH = D_MODEL // 2
GMLP_GROUPS = 8
GMLP_GROUP_DIM = GMLP_WIDTH // GMLP_GROUPS
GMLP_CHUNK = 128
PEER_HEADS = 8
PEER_NKEYS = 128
PEER_EXPERTS = PEER_NKEYS * PEER_NKEYS
PEER_QDIM = 128
PEER_HALF = PEER_QDIM // 2
PEER_TOPK = 16
PEER_TOKCHUNK = 128
IN_WIDTH = 3 * ATTN_WIDTH + 2 * GMLP_WIDTH + 2 * D_MODEL
NORM_EPS = 1e-6
NEG_INF = -1e30

kernel_name = "hybrid_moba_gmlp_peer_block"

def rms_norm(x, g):
    xf = x.astype(jnp.float32)
    y = xf * lax.rsqrt(jnp.mean(xf * xf, axis=-1, keepdims=True) + NORM_EPS)
    return (y * g.astype(jnp.float32)).astype(x.dtype)

def layer_norm(x, g, b):
    xf = x.astype(jnp.float32)
    mu = jnp.mean(xf, axis=-1, keepdims=True)
    xc = xf - mu
    var = jnp.mean(xc * xc, axis=-1, keepdims=True)
    y = xc * lax.rsqrt(var + NORM_EPS) * g.astype(jnp.float32) + b.astype(jnp.float32)
    return y.astype(x.dtype)

def t5_bucket(rel):
    max_exact = REL_BUCKETS // 2
    n = jnp.maximum(rel, 0)
    nf = jnp.maximum(n, max_exact).astype(jnp.float32)
    large = max_exact + (jnp.log(nf / max_exact) / math.log(REL_MAX_DISTANCE / max_exact)
                         * (REL_BUCKETS - max_exact)).astype(jnp.int32)
    large = jnp.minimum(large, REL_BUCKETS - 1)
    return jnp.where(n < max_exact, n, large)

def moba_attention(q, k, v, rel_bias):
    B, S, H, dh = q.shape
    nb = -(-S // MOBA_BLOCK)
    pad = nb * MOBA_BLOCK - S
    q = q.transpose(0, 2, 1, 3)
    k = jnp.pad(k.transpose(0, 2, 1, 3), ((0, 0), (0, 0), (0, pad), (0, 0)))
    v = jnp.pad(v.transpose(0, 2, 1, 3), ((0, 0), (0, 0), (0, pad), (0, 0)))
    kb = k.reshape(B, H, nb, MOBA_BLOCK, dh)
    vb = v.reshape(B, H, nb, MOBA_BLOCK, dh)
    scale = dh ** -0.5
    q_blk = jnp.arange(S) // MOBA_BLOCK
    n_slots = min(MOBA_TOPK, nb - 1)
    if n_slots > 0:
        k_mean = jnp.mean(kb.astype(jnp.float32), axis=3)
        score = jnp.einsum('bhsd,bhnd->bhsn', q.astype(jnp.float32), k_mean)
        fully_past = jnp.arange(nb)[None, :] < q_blk[:, None]
        score = jnp.where(fully_past, score, NEG_INF)
        _, sel = lax.top_k(score, n_slots)
    else:
        sel = jnp.zeros((B, H, S, 0), jnp.int32)
    sel_valid = jnp.arange(n_slots)[None, :] < q_blk[:, None]

    nc = S // MOBA_QCHUNK
    q_c = q.reshape(B, H, nc, MOBA_QCHUNK, dh).transpose(2, 0, 1, 3, 4)
    sel_c = sel.reshape(B, H, nc, MOBA_QCHUNK, n_slots).transpose(2, 0, 1, 3, 4)
    valid_c = sel_valid.reshape(nc, MOBA_QCHUNK, n_slots)
    rb = rel_bias.T.astype(jnp.float32)
    b_ix = jnp.arange(B)[:, None, None]
    h_ix = jnp.arange(H)[None, :, None]
    offs = jnp.arange(MOBA_BLOCK)

    def one_chunk(args):
        qc, selc, validc, ci = args
        q_pos = ci * MOBA_QCHUNK + jnp.arange(MOBA_QCHUNK)
        own = (ci * MOBA_QCHUNK) // MOBA_BLOCK
        k_own = lax.dynamic_index_in_dim(kb, own, axis=2, keepdims=False)
        v_own = lax.dynamic_index_in_dim(vb, own, axis=2, keepdims=False)
        rel = q_pos[:, None] - (own * MOBA_BLOCK + offs)[None, :]
        lg = (jnp.einsum('bhqd,bhkd->bhqk', qc, k_own).astype(jnp.float32) * scale
              + rb[:, t5_bucket(rel)])
        logits = [jnp.where(rel >= 0, lg, NEG_INF)]
        for j in range(n_slots):
            idx = selc[..., j]
            k_j = kb[b_ix, h_ix, idx]
            rel_j = q_pos[:, None] - (idx[..., None] * MOBA_BLOCK + offs)
            lg = (jnp.einsum('bhqd,bhqkd->bhqk', qc, k_j).astype(jnp.float32) * scale
                  + rb[h_ix[..., None], t5_bucket(rel_j)])
            logits.append(jnp.where(validc[:, j][:, None], lg, NEG_INF))
        p = jax.nn.softmax(jnp.concatenate(logits, axis=-1), axis=-1).astype(vb.dtype)
        out = jnp.einsum('bhqk,bhkd->bhqd', p[..., :MOBA_BLOCK], v_own)
        for j in range(n_slots):
            v_j = vb[b_ix, h_ix, selc[..., j]]
            out = out + jnp.einsum('bhqk,bhqkd->bhqd',
                                   p[..., (j + 1) * MOBA_BLOCK:(j + 2) * MOBA_BLOCK], v_j)
        return out

    out = lax.map(one_chunk, (q_c, sel_c, valid_c, jnp.arange(nc)))
    return out.transpose(1, 0, 3, 2, 4).reshape(B, S, H * dh)

def spatial_gating(z_u, z_v, ln_g, ln_b, w_s, b_s):
    B, S, _ = z_u.shape
    u = jax.nn.gelu(z_u)
    v = layer_norm(jax.nn.gelu(z_v), ln_g, ln_b)
    nch = S // GMLP_CHUNK
    vc = v.reshape(B, nch, GMLP_CHUNK, GMLP_GROUPS, GMLP_GROUP_DIM)
    causal = jnp.tril(jnp.ones((GMLP_CHUNK, GMLP_CHUNK), dtype=bool))
    w = jnp.where(causal, w_s, jnp.zeros((), w_s.dtype)).astype(v.dtype)
    mixed = jnp.einsum('gts,bnsgc->bntgc', w, vc) + b_s.T[:, :, None].astype(v.dtype)
    return u * mixed.reshape(B, S, GMLP_WIDTH)

def token_mixing(h, w_in, gmlp_ln_g, gmlp_ln_b, gmlp_w_s, gmlp_b_s, rel_bias,
                 w_branch_attn, w_branch_gmlp, w_out):
    B, S, _ = h.shape
    proj = h @ w_in
    a3 = 3 * ATTN_WIDTH
    cuts = [ATTN_WIDTH, 2 * ATTN_WIDTH, a3, a3 + GMLP_WIDTH, a3 + 2 * GMLP_WIDTH,
            a3 + 2 * GMLP_WIDTH + D_MODEL]
    q, k, v, z_u, z_v, g_attn, g_gmlp = jnp.split(proj, cuts, axis=-1)
    heads = (B, S, ATTN_HEADS, HEAD_DIM)
    y_attn = moba_attention(q.reshape(heads), k.reshape(heads), v.reshape(heads), rel_bias)
    y_gmlp = spatial_gating(z_u, z_v, gmlp_ln_g, gmlp_ln_b, gmlp_w_s, gmlp_b_s)
    merged = (jax.nn.sigmoid(g_attn) * (y_attn @ w_branch_attn)
              + jax.nn.sigmoid(g_gmlp) * (y_gmlp @ w_branch_gmlp))
    return merged @ w_out

def peer_ffn(h, w_query, sub_keys, expert_u, expert_v):
    B, S, D = h.shape
    T = B * S
    x = h.reshape(T, D)
    q = (x @ w_query).reshape(T, PEER_HEADS, 2, PEER_HALF).astype(jnp.float32)
    sk = sub_keys.astype(jnp.float32)
    s1 = jnp.einsum('thd,kd->thk', q[:, :, 0], sk[0])
    s2 = jnp.einsum('thd,kd->thk', q[:, :, 1], sk[1])
    v1, i1 = lax.top_k(s1, PEER_TOPK)
    v2, i2 = lax.top_k(s2, PEER_TOPK)
    cand = (v1[..., :, None] + v2[..., None, :]).reshape(T, PEER_HEADS, PEER_TOPK * PEER_TOPK)
    sc, flat = lax.top_k(cand, PEER_TOPK)
    e = (jnp.take_along_axis(i1, flat // PEER_TOPK, axis=-1) * PEER_NKEYS
         + jnp.take_along_axis(i2, flat % PEER_TOPK, axis=-1))
    g = jax.nn.softmax(sc, axis=-1).astype(h.dtype)
    nchunk = T // PEER_TOKCHUNK

    def one_chunk(args):
        xc, ec, gc = args
        u = expert_u[ec]
        a = jax.nn.gelu(jnp.einsum('cd,chkd->chk', xc, u))
        return jnp.einsum('chk,chkd->cd', gc * a, expert_v[ec])

    out = lax.map(one_chunk, (x.reshape(nchunk, PEER_TOKCHUNK, D),
                              e.reshape(nchunk, PEER_TOKCHUNK, PEER_HEADS, PEER_TOPK),
                              g.reshape(nchunk, PEER_TOKCHUNK, PEER_HEADS, PEER_TOPK)))
    return out.reshape(B, S, D)

def setup_inputs(seed: int = 0) -> dict:
    key = jax.random.key(seed)
    ks = jax.random.split(key, 24)
    f32 = jnp.float32
    L = DEPTH

    def nrm(k, shape, scale):
        return jax.random.normal(k, shape, f32) * scale

    return {
        "x": nrm(ks[0], (BATCH, SEQ, D_MODEL), 1.0),
        "c": nrm(ks[1], (BATCH, D_MODEL), 1.0),
        "ada_w": nrm(ks[2], (L, D_MODEL, 6 * D_MODEL), 0.5 * D_MODEL ** -0.5),
        "ada_b": nrm(ks[3], (L, 6 * D_MODEL), 0.02),
        "pre_g1": 1.0 + nrm(ks[4], (L, D_MODEL), 0.02),
        "post_g1": 1.0 + nrm(ks[5], (L, D_MODEL), 0.02),
        "w_in": nrm(ks[6], (L, D_MODEL, IN_WIDTH), D_MODEL ** -0.5),
        "gmlp_ln_g": 1.0 + nrm(ks[7], (L, GMLP_WIDTH), 0.02),
        "gmlp_ln_b": nrm(ks[8], (L, GMLP_WIDTH), 0.02),
        "gmlp_w_s": nrm(ks[9], (L, GMLP_GROUPS, GMLP_CHUNK, GMLP_CHUNK), GMLP_CHUNK ** -0.5),
        "gmlp_b_s": 1.0 + nrm(ks[10], (L, GMLP_GROUPS, GMLP_CHUNK), 0.02),
        "rel_bias": nrm(ks[11], (REL_BUCKETS, ATTN_HEADS), 0.5),
        "w_branch_attn": nrm(ks[12], (L, ATTN_WIDTH, D_MODEL), ATTN_WIDTH ** -0.5),
        "w_branch_gmlp": nrm(ks[13], (L, GMLP_WIDTH, D_MODEL), GMLP_WIDTH ** -0.5),
        "w_out": nrm(ks[14], (L, D_MODEL, D_MODEL), D_MODEL ** -0.5),
        "pre_g2": 1.0 + nrm(ks[15], (L, D_MODEL), 0.02),
        "post_g2": 1.0 + nrm(ks[16], (L, D_MODEL), 0.02),
        "peer_w_query": nrm(ks[17], (L, D_MODEL, PEER_HEADS * PEER_QDIM), D_MODEL ** -0.5),
        "peer_sub_keys": nrm(ks[18], (L, 2, PEER_NKEYS, PEER_HALF), PEER_HALF ** -0.5),
        "peer_u": nrm(ks[19], (L, PEER_EXPERTS, D_MODEL), D_MODEL ** -0.5),
        "peer_v": nrm(ks[20], (L, PEER_EXPERTS, D_MODEL), D_MODEL ** -0.5),
    }

def reference(x, c, ada_w, ada_b, pre_g1, post_g1, w_in, gmlp_ln_g, gmlp_ln_b,
              gmlp_w_s, gmlp_b_s, rel_bias, w_branch_attn, w_branch_gmlp, w_out,
              pre_g2, post_g2, peer_w_query, peer_sub_keys, peer_u, peer_v):
    cond = jax.nn.silu(c)
    for l in range(DEPTH):
        mod = cond @ ada_w[l] + ada_b[l]
        sh1, sc1, gt1, sh2, sc2, gt2 = jnp.split(mod[:, None, :], 6, axis=-1)
        h = rms_norm(x, pre_g1[l]) * (1.0 + sc1) + sh1
        y = token_mixing(h, w_in[l], gmlp_ln_g[l], gmlp_ln_b[l], gmlp_w_s[l], gmlp_b_s[l],
                         rel_bias, w_branch_attn[l], w_branch_gmlp[l], w_out[l])
        x = x + gt1 * rms_norm(y, post_g1[l])
        h = rms_norm(x, pre_g2[l]) * (1.0 + sc2) + sh2
        y = peer_ffn(h, peer_w_query[l], peer_sub_keys[l], peer_u[l], peer_v[l])
        x = x + gt2 * rms_norm(y, post_g2[l])
    return x


_drawn_inputs = setup_inputs


def setup_inputs(seed=0):
    import zlib

    import numpy as np

    out = dict(_drawn_inputs(seed))
    spreads = {}
    factors = {'gmlp_ln_g': 3.466, 'gmlp_ln_b': 3.648, 'gmlp_b_s': 2.87, 'post_g2': 8.0}
    for name, (base, spread) in spreads.items():
        noise = np.random.default_rng([zlib.crc32(name.encode()), seed]).standard_normal(out[name].shape)
        drawn = base * np.exp(spread * noise) if base else spread * noise
        out[name] = jnp.asarray(drawn.astype(out[name].dtype))
    for name, factor in factors.items():
        out[name] = (out[name] * factor).astype(out[name].dtype)
    return out
```

```python
from contextlib import ExitStack
import math

import numpy as np

import concourse.bass as bass
from concourse import mybir

P = 128
D = 1024
S = 512
NT = S // P
KD = D // P
HALF = 512
H, DH = 8, 64
AW = H * DH
GW = D // 2
G, GD = 8, 64
BUCKETS, MAX_DIST = 32, 2048
PH, NK, QD = 8, 128, 128
TOPK = 16
EPS = 1e-6
NEG = -1e30
LOWEST = -3.0e38

F32 = mybir.dt.float32
U32 = mybir.dt.uint32
ALU = mybir.AluOpType
ACT = mybir.ActivationFunctionType
AX = mybir.AxisListType.X

N_ADA, N_IN = 6 * D // HALF, (3 * AW + 2 * GW + 2 * D) // HALF
BLK_ADA, BLK_IN = 0, N_ADA
BLK_BRANCH = BLK_IN + N_IN
BLK_OUT = BLK_BRANCH + 2
BLK_QUERY = BLK_OUT + 2
N_BLK = BLK_QUERY + 2
RING = 3
GRP = 4
NGRP = TOPK // GRP
UNITS = NT * PH
UNIT_TICKS = 36


def bucket_onehot():
    n = (S - 1) - np.arange(2 * S)
    exact = BUCKETS // 2
    nf = np.maximum(n, exact).astype(np.float32)
    large = exact + (np.log(nf / np.float32(exact)) / np.float32(math.log(MAX_DIST / exact))
                     * np.float32(BUCKETS - exact)).astype(np.int32)
    b = np.where(n < exact, n, np.minimum(large, BUCKETS - 1))
    hot = (np.arange(BUCKETS)[:, None] == b[None, :]) & (n >= 0)[None, :]
    return np.concatenate([hot, (n < 0)[None, :]]).astype(np.float32)



JOBS = {}
for _names in (
    [("ext", f) for f in range(2)],
    [("ada", b) for b in range(N_ADA)],
    [("hT", t, f) for t in range(NT) for f in range(2)],
    [("bt", h) for h in range(H)],
    [("in", b, j) for b in range(N_IN) for j in range(4)],
    [("mix", q) for q in range(4)], [("gT", t) for t in range(NT)],
    [("s", 0, i) for i in range(NT)],
    [job for h in range(H) for job in
     [("s", h + 1, i) for i in range(NT) if h + 1 < H] + [("pT", h, i) for i in range(NT)] + [("pv", h)]],
    [(a, t, f) for t in range(NT) for f in range(2) for a in ("ba", "bg")],
    [("mT", t, f) for t in range(NT) for f in range(2)],
    [("y", t, f) for t in range(NT) for f in range(2)],
    [("h2T", t, f) for t in range(NT) for f in range(2)],
    [("pq", h) for h in range(PH)],
    [("sc", t, q) for t in range(NT) for q in range(PH // 2)],
):
    for _n in _names:
        JOBS[_n] = len(JOBS)


def build(nc, x, c, ada_w, ada_b, rows_g, w_in, ln_gb, w_s, b_s, rel, w_branch, w_out, w_query, keys,
          u_exp, v_exp, hot, ident_in, anti_in, out):
    bias_dram = nc.dram_tensor("bias_scratch", [H, 2 * S], F32, kind="Internal").ap()
    ctx = ExitStack()
    with ctx:
        def sb(name, shape, dt=F32):
            return ctx.enter_context(nc.sbuf_tensor(name, shape, dt))

        def sem(name):
            return ctx.enter_context(nc.semaphore(name))

        xr = sb("xr", [P, NT, D])
        nat = sb("nat", [P, NT, D])
        mods = sb("mods", [P, 6, D])
        cond = sb("cond", [P, KD, P])
        ident = sb("ident", [P, P])
        probs = sb("probs", [P, 2, 1280])
        small = sb("small", [P, 256])
        arena = sb("arena", [P, 136 * 256])

        def part(start_kb, *shape):
            n = math.prod(shape)
            a = arena[:, int(start_kb * 256):int(start_kb * 256) + n]
            if len(shape) == 1:
                return a
            if len(shape) == 2:
                return a.rearrange("p (a b) -> p a b", a=shape[0])
            return a.rearrange("p (a b c) -> p a b c", a=shape[0], b=shape[1])

        ring = part(0, RING, KD, HALF)
        hT = part(48, KD, S)
        qT, kT, va = part(64, NT, S), part(72, NT, S), part(80, NT, S)
        zu, zv = part(88, NT, S), part(96, NT, S)
        ga, gg = part(104, NT, D), part(120, NT, D)
        gains = ga
        bias = nat[:, :, :].rearrange("p t d -> p (t d)").rearrange("p (h m) -> p h m", h=H)
        flipped = part(120, H, S)
        anti = part(72, P)
        wsT = cond
        pT = part(48, 2, NT, S)
        yaT, ygT, mT = qT, zv, hT
        junk = part(88, D)
        ln_row = probs[:, 0, 0:2 * GW].rearrange("p (a d) -> p a d", a=2)
        ext = probs[0:H, 0, 0:2 * S]
        hot_sb = probs[0:BUCKETS + 1, 1, 0:2 * S]

        h2, h2T, pqT = ga, hT, part(120, PH, S)
        skb = part(64, 2 * NK)
        scores = part(65, UNITS + 1, 2 * NK)
        urows = part(0, TOPK, D)
        vrows = [part(120, 4, D)[:, s, :] for s in range(4)] + [mods[:, s, :] for s in range(4)]
        cur = part(98, 2, NK)
        cand = part(99, TOPK, TOPK)
        match = part(100, 2 * TOPK, TOPK)
        spot = part(102, 512)
        top = spot[:, 0:32].rearrange("p (a k) -> p a k", a=2)
        top_i = spot[:, 32:64].bitcast(U32).rearrange("p (a k) -> p a k", a=2)
        top_f = spot[:, 64:96].rearrange("p (a k) -> p a k", a=2)
        best = spot[:, 96:112]
        best_i = spot[:, 112:128].bitcast(U32)
        pair_i = spot[:, 128:160].bitcast(U32).rearrange("p (a k) -> p a k", a=2)
        pair_f = spot[:, 160:192]
        key = spot[:, 192:224]
        shifted = [spot[:, 224 + 16 * p:240 + 16 * p] for p in range(2)]
        idx = [spot[:, 256 + 16 * p:272 + 16 * p].bitcast(U32) for p in range(2)]
        expd = [spot[:, 288 + 16 * p:304 + 16 * p] for p in range(2)]
        act_in = [spot[:, 320 + 16 * p:336 + 16 * p] for p in range(2)]
        act_out = [spot[:, 352 + 16 * p:368 + 16 * p] for p in range(2)]
        coef = [spot[:, 384 + 16 * p:400 + 16 * p] for p in range(2)]
        esum = [spot[:, 416 + p:417 + p] for p in range(2)]
        einv = [spot[:, 418 + p:419 + p] for p in range(2)]
        iota_f = spot[:, 432:448]

        def cols(a, n=1):
            return small[:, a:a + n]

        sumsq, ms, rstd = (lambda k, t: cols(4 * k + t)), (lambda k, t: cols(16 + 4 * k + t)), \
            (lambda k, t: cols(32 + 4 * k + t))
        mhalf = cols(48)
        bs = cols(52, G)
        bn, mv = (lambda t: cols(60 + 6 * t, 6)), (lambda t: cols(84 + 2 * t, 2))
        v_ms, v_rstd = (lambda t: cols(92 + t)), (lambda t: cols(96 + t))
        mx, nmx, rsum, rinv = (lambda h, i: cols(100 + 4 * (h % 4) + i)), (lambda h, i: cols(116 + 4 * (h % 4) + i)), \
            (lambda h, i: cols(132 + 4 * (h % 4) + i)), (lambda h, i: cols(148 + 4 * (h % 4) + i))
        ccol, ecol, scol = cols(164, KD), cols(172, KD), cols(180, KD)
        rel_sb = small[0:BUCKETS + 1, 188:188 + H]
        iota_i = small[:, 200:216].bitcast(mybir.dt.int32)

        def prob(h, i):
            at = [0, 128, 384, 768][i]
            return probs[:, h % 2, at:at + P * (i + 1)]

        banks = [ctx.enter_context(nc.psum_tensor(f"bank{i}", [P, HALF], F32)) for i in range(8)]
        bank_full = [sem(f"bank_full{i}") for i in range(8)]
        bank_free = [sem(f"bank_free{i}") for i in range(8)]

        def bank(*job):
            return banks[JOBS[job] % 8]

        def take(eng, *job):
            eng.wait_ge(bank_full[JOBS[job] % 8], JOBS[job] // 8 + 1)
            return bank(*job)

        def free(*job):
            return bank_free[JOBS[job] % 8]

        def last_of(jobs):
            return {n % 8: n // 8 + 1 for n in sorted(JOBS[job] for job in jobs)}

        def stored(eng, *jobs):
            for b, n in last_of(jobs).items():
                eng.wait_ge(bank_free[b], n)

        def multiplied(eng, *jobs):
            for b, n in last_of(jobs).items():
                eng.wait_ge(bank_full[b], n)

        def group(kind):
            return [j for j in JOBS if j[0] == kind]

        x_in = [sem(f"x_in{t}") for t in range(NT)]
        c_in, ada_b_in, gains_in, ident_landed, ln_in, ws_in, bs_in = (
            sem(n) for n in ("c_in", "ada_b_in", "gains_in", "ident_landed", "ln_in", "ws_in", "bs_in"))
        hot_in, rel_in, rel_mask, bias_out, bias_in, keys_in = (
            sem(n) for n in ("hot_in", "rel_in", "rel_mask", "bias_out", "bias_in", "keys_in"))
        blk_in = [sem(f"blk_in{r}") for r in range(RING)]
        cond_exp, cond_ready, sq_ready, rstd_ready, pool_const, pool_chain, dve_chain = (
            sem(n) for n in ("cond_exp", "cond_ready", "sq_ready", "rstd_ready", "pool_const", "pool_chain",
                             "dve_chain"))
        h_ready, v_var, v_rs, v_normed, ws_masked, yg_ready, max_ready, exp_ready, p_ready = (
            sem(n) for n in ("h_ready", "v_var", "v_rs", "v_normed", "ws_masked", "yg_ready", "max_ready",
                             "exp_ready", "p_ready"))
        merged, x_new, h2_ready, idx_ready, shift_ready, soft_ready, dots_ready, gelu_ready = (
            sem(n) for n in ("merged", "x_new", "h2_ready", "idx_ready", "shift_ready", "soft_ready",
                             "dots_ready", "gelu_ready"))
        u_in = [sem(f"u_in{g}") for g in range(NGRP)]
        v_in = [sem(f"v_in{r}") for r in range(2)]
        u_free, v_free, summed, out_ready, out_stored = (
            sem(n) for n in ("u_free", "v_free", "summed", "out_ready", "out_stored"))
        dve_tick, dve_passed, pool_passed = sem("dve_tick"), sem("dve_passed"), sem("pool_passed")

        def blk(n):
            return ring[:, n % RING]

        w_src = []
        for b in range(N_ADA):
            w_src.append(ada_w[:, b * HALF:(b + 1) * HALF].rearrange("(k p) n -> p k n", p=P))
        for b in range(N_IN):
            w_src.append(w_in[:, b * HALF:(b + 1) * HALF].rearrange("(k p) n -> p k n", p=P))
        for b in range(2):
            w_src.append(w_branch[:, b * HALF:(b + 1) * HALF].rearrange("(k p) n -> p k n", p=P))
        for w in (w_out, w_query):
            for b in range(2):
                w_src.append(w[:, b * HALF:(b + 1) * HALF].rearrange("(k p) n -> p k n", p=P))

        last_reader = [("ada", b) for b in range(N_ADA)] + [("in", b, 3) for b in range(N_IN)] \
            + [("bg", NT - 1, 0), ("bg", NT - 1, 1), ("y", NT - 1, 0), ("y", NT - 1, 1), ("pq", 3), ("pq", 7)]

        block = ctx.enter_context(nc.Block())

        @block.sync
        def _(sp):
            sp.dma_start(ccol, c).then_inc(c_in, 16)
            sp.dma_start(hot_sb, hot).then_inc(hot_in, 16)
            sp.wait_ge(rel_mask, 1)
            sp.dma_start(rel_sb[0:BUCKETS, :], rel).then_inc(rel_in, 16)
            for n in range(N_BLK):
                if n >= RING:
                    multiplied(sp, last_reader[n - RING])
                sp.dma_start(blk(n), w_src[n]).then_inc(blk_in[n % RING], 16)
                if n == 1:
                    sp.dma_start(mods[:, :, :].rearrange("p a d -> p (a d)"),
                                 ada_b.partition_broadcast(P)).then_inc(ada_b_in, 16)
                if n == 2:
                    sp.dma_start(ident[:, :], ident_in).then_inc(ident_landed, 16)
                    sp.dma_start(anti, anti_in).then_inc(ident_landed, 16)
                    sp.dma_start(gains[:, :, :].rearrange("p a d -> p (a d)"),
                                 rows_g.partition_broadcast(P)).then_inc(gains_in, 16)
                    for t in range(NT):
                        sp.dma_start(xr[:, t, :], x[0, t * P:(t + 1) * P, :]).then_inc(x_in[t], 16)
                    sp.dma_start(bs, b_s).then_inc(bs_in, 16)
            for t in range(NT):
                sp.wait_ge(out_ready, t + 1)
                sp.dma_start(out[0, t * P:(t + 1) * P, :], nat[:, t, :]).then_inc(out_stored, 16)
            sp.wait_ge(out_stored, 16 * NT)

        @block.gpsimd
        def _(pool):
            chain = [0]

            def link(ins):
                chain[0] += 1
                ins.then_inc(pool_chain, 1)
                pool.wait_ge(pool_chain, chain[0])

            def norm(k, t):
                pool.wait_ge(sq_ready, NT * k + t + 1)
                link(pool.tensor_scalar(ms(k, t), sumsq(k, t), 1.0 / D, EPS, ALU.mult, ALU.add))
                pool.tensor_tensor(rstd(k, t), ms(k, t), mhalf, ALU.pow).then_inc(rstd_ready, 1)

            pool.memset(rel_sb, NEG).then_inc(rel_mask, 1)
            link(pool.memset(mhalf, -0.5))
            link(pool.iota(iota_i, pattern=[[1, TOPK]], base=0, channel_multiplier=0))
            stored(pool, ("ext", 0), ("ext", 1))
            pool.dma_start(bias_dram, ext).then_inc(bias_out, 16)
            for t in range(NT):
                norm(0, t)
            pool.wait_ge(bias_out, 16)
            pool.dma_start(flipped, bass.AP(bias_dram.tensor, 0, [[1, P], [2 * S, H], [1, S]]))\
                .then_inc(bias_in, 16)
            pool.dma_start(ln_row, ln_gb.partition_broadcast(P)).then_inc(ln_in, 16)
            multiplied(pool, *group("ada"))
            pool.dma_start(wsT[:, :, :], w_s).then_inc(ws_in, 16)
            pool.wait_ge(ws_in, 16)
            pool.affine_select(out=wsT[:, :, :], in_=wsT[:, :, :], compare_op=ALU.is_ge, fill=0.0, base=0,
                               pattern=[[0, G], [1, P]], channel_multiplier=-1).then_inc(ws_masked, 1)
            for t in range(NT):
                pool.wait_ge(v_var, t + 1)
                link(pool.tensor_scalar(v_ms(t), mv(t)[:, 1:2], 1.0, EPS, ALU.mult, ALU.add))
                pool.tensor_tensor(v_rstd(t), v_ms(t), mhalf, ALU.pow).then_inc(v_rs, 1)
            multiplied(pool, *group("ba"))
            pool.dma_start(skb, keys).then_inc(keys_in, 16)
            for k in (1, 2):
                for t in range(NT):
                    norm(k, t)

            def gather(table, row, ix, signal):
                pool.indirect_dma_start(out=row, out_offset=None, in_=table,
                                        in_offset=bass.IndirectOffsetOnAxis(ap=ix, axis=0)).then_inc(signal, 16)

            def wait_apart(signal, n):
                pool.wait_ge(signal, n)
                pool.nop().then_inc(pool_passed, 1)

            with pool.Fori(0, UNITS // 2) as i:
                for p in range(2):
                    n = i * 2 + p
                    pool.wait_ge(idx_ready, n + 1)
                    for g in range(NGRP):
                        wait_apart(u_free, n * NGRP + (g + 1))
                        for s in range(g * GRP, (g + 1) * GRP):
                            gather(u_exp, urows[:, s, :], idx[p][:, s:s + 1], u_in[g])
                    for g in range(NGRP):
                        wait_apart(v_free, n * NGRP + (g + 1))
                        for s in range(g * GRP, (g + 1) * GRP):
                            gather(v_exp, vrows[s % 8], idx[p][:, s:s + 1], v_in[g % 2])
            for t in range(NT):
                norm(3, t)

        @block.tensor
        def _(pe):
            def start(*job):
                if JOBS[job] >= 8:
                    pe.wait_ge(free(*job), JOBS[job] // 8)
                return bank(*job)

            def full(last, *job):
                last.then_inc(bank_full[JOBS[job] % 8], 1)

            def arrived(n):
                pe.wait_ge(blk_in[n % RING], 16 * (n // RING + 1))
                return blk(n)

            def product(job, pairs):
                o = start(*job)
                for k, (a, b) in enumerate(pairs):
                    last = pe.matmul(o[:, :], a, b, start=(k == 0), stop=(k == len(pairs) - 1))
                full(last, *job)

            def transposes(job, blocks):
                o = start(*job)
                for k, a in enumerate(blocks):
                    last = pe.transpose(o[:, k * P:(k + 1) * P], a, ident[:, :])
                full(last, *job)

            pe.wait_ge(hot_in, 16)
            pe.wait_ge(rel_in, 16)
            for f in range(2):
                o = start("ext", f)
                full(pe.matmul(o[0:H, :], rel_sb, hot_sb[:, f * HALF:(f + 1) * HALF], start=True, stop=True),
                     "ext", f)
            pe.wait_ge(cond_ready, KD)
            for b in range(N_ADA):
                w = arrived(BLK_ADA + b)
                product(("ada", b), [(cond[:, k, :], w[:, k, :]) for k in range(KD)])
            pe.wait_ge(ident_landed, 32)
            for t in range(NT):
                pe.wait_ge(h_ready, t + 1)
                for f in range(2):
                    transposes(("hT", t, f), [nat[:, t, (4 * f + k) * P:(4 * f + k + 1) * P] for k in range(4)])
            pe.wait_ge(bias_in, 16)
            pe.wait_ge(ident_landed, 32)
            for h in range(H):
                product(("bt", h), [(anti, flipped[:, h, :])])
            stored(pe, *group("hT"))
            for b in range(N_IN):
                w = arrived(BLK_IN + b)
                for j in range(4):
                    cut = slice(j * P, (j + 1) * P)
                    product(("in", b, j), [(w[:, k, cut], hT[:, k, :]) if b < 2 else (hT[:, k, cut], w[:, k, :])
                                           for k in range(KD)])
            pe.wait_ge(ws_masked, 1)
            pe.wait_ge(v_normed, NT)
            for q in range(4):
                o = start("mix", q)
                for e in range(2):
                    g = 2 * q + e
                    last = pe.matmul(o[:, e * 256:(e + 1) * 256], wsT[:, g, :], zv[:, :, g * GD:(g + 1) * GD],
                                     start=True, stop=True)
                full(last, "mix", q)
            pe.wait_ge(yg_ready, G)
            for t in range(NT):
                transposes(("gT", t), [zu[:, t, k * P:(k + 1) * P] for k in range(4)])

            def logits(h):
                r0 = DH * (h % 2)
                for i in range(NT):
                    o = start("s", h, i)
                    w = P * (i + 1)
                    full(pe.matmul(o[:, 0:w], qT[r0:r0 + DH, h // 2, i * P:(i + 1) * P],
                                   kT[r0:r0 + DH, h // 2, 0:w], start=True, stop=True), "s", h, i)

            stored(pe, *group("in"))
            logits(0)
            for h in range(H):
                if h + 1 < H:
                    logits(h + 1)
                for i in range(NT):
                    pe.wait_ge(p_ready, NT * h + i + 1)
                    transposes(("pT", h, i), [prob(h, i)[:, j * P:(j + 1) * P] for j in range(i + 1)])
                stored(pe, *[("pT", h, i) for i in range(NT)])
                o = start("pv", h)
                r0 = DH * (h % 2)
                for j in range(NT):
                    last = pe.matmul(o[r0:r0 + DH, j * P:S], va[:, j, h * DH:(h + 1) * DH],
                                     pT[:, h % 2, j, j * P:S], start=(j == 0), stop=(j == NT - 1))
                full(last, "pv", h)
            stored(pe, *group("pv"), *group("gT"))
            wb = [arrived(BLK_BRANCH), arrived(BLK_BRANCH + 1)]
            for t in range(NT):
                cut = slice(t * P, (t + 1) * P)
                for f in range(2):
                    product(("ba", t, f), [(yaT[:, k, cut], wb[f][:, k, :]) for k in range(4)])
                    product(("bg", t, f), [(ygT[:, k, cut], wb[f][:, 4 + k, :]) for k in range(4)])
            for t in range(NT):
                for f in range(2):
                    pe.wait_ge(merged, 2 * t + f + 1)
                    transposes(("mT", t, f), [ga[:, t, (4 * f + k) * P:(4 * f + k + 1) * P] for k in range(4)])
            wo = [arrived(BLK_OUT), arrived(BLK_OUT + 1)]
            for t in range(NT):
                stored(pe, ("mT", t, 0), ("mT", t, 1))
                for f in range(2):
                    product(("y", t, f), [(mT[:, k, t * P:(t + 1) * P], wo[f][:, k, :]) for k in range(KD)])
            for t in range(NT):
                pe.wait_ge(h2_ready, t + 1)
                for f in range(2):
                    transposes(("h2T", t, f), [h2[:, t, (4 * f + k) * P:(4 * f + k + 1) * P] for k in range(4)])
            stored(pe, *group("h2T"))
            for b in range(2):
                w = arrived(BLK_QUERY + b)
                for j in range(4):
                    product(("pq", 4 * b + j), [(w[:, k, j * P:(j + 1) * P], h2T[:, k, :]) for k in range(KD)])
            pe.wait_ge(keys_in, 16)
            stored(pe, *group("pq"))
            for t in range(NT):
                for q in range(4):
                    o = start("sc", t, q)
                    for e in range(2):
                        last = pe.matmul(o[:, e * 256:(e + 1) * 256], pqT[:, 2 * q + e, t * P:(t + 1) * P], skb,
                                         start=True, stop=True)
                    full(last, "sc", t, q)

        @block.scalar
        def _(act):
            def quads(a, t, f):
                return a[:, 4 * f:4 * f + 4, t * P:(t + 1) * P]

            def four(o):
                return o[:, :].rearrange("p (k t) -> p k t", k=4)

            def squares(k, t, a, spare):
                if NT * k + t:
                    act.wait_ge(sq_ready, NT * k + t)
                act.activation(spare, a, ACT.Square, accum_out=sumsq(k, t)).then_inc(sq_ready, 1)

            act.wait_ge(c_in, 16)
            act.activation(ecol, ccol, ACT.Exp, scale=-1.0).then_inc(cond_exp, 1)
            for f in range(2):
                o = take(act, "ext", f)
                act.activation(ext[:, f * HALF:(f + 1) * HALF], o[0:H, :], ACT.Copy).then_inc(free("ext", f), 1)
            for t in range(NT):
                act.wait_ge(x_in[t], 16)
                squares(0, t, xr[:, t, :], junk)
            for t in range(NT):
                for f in range(2):
                    o = take(act, "hT", t, f)
                    act.activation(quads(hT, t, f), four(o), ACT.Copy).then_inc(free("hT", t, f), 1)
            for h in range(H):
                o = take(act, "bt", h)
                act.activation(bias[:, h, :], o[:, :], ACT.Copy).then_inc(free("bt", h), 1)
            act.wait_ge(sq_ready, NT)
            for b in range(N_IN):
                for j in range(4):
                    if b == 2:
                        continue
                    if b == 5 and j == 0:
                        multiplied(act, *group("hT"))
                        act.wait_ge(h_ready, NT)
                    o = take(act, "in", b, j)
                    done = free("in", b, j)
                    if b == 0:
                        act.activation(qT[:, j, :], o[:, :], ACT.Copy, scale=DH ** -0.5).then_inc(done, 1)
                    elif b == 1:
                        act.activation(kT[:, j, :], o[:, :], ACT.Copy).then_inc(done, 1)
                    elif b == 3:
                        act.activation(zu[:, j, :], o[:, :], ACT.Gelu_apprx_tanh).then_inc(done, 1)
                    elif b == 4:
                        act.activation(zv[:, j, :], o[:, :], ACT.Gelu_apprx_tanh).then_inc(done, 1)
                    else:
                        gate, f = (ga, b - 5) if b < 7 else (gg, b - 7)
                        act.activation(gate[:, j, f * HALF:(f + 1) * HALF], o[:, :], ACT.Tanh, scale=0.5)\
                            .then_inc(done, 1)
            for t in range(NT):
                if t == 0:
                    multiplied(act, *group("mix"))
                o = take(act, "gT", t)
                act.activation(ygT[:, :, t * P:(t + 1) * P], four(o), ACT.Copy).then_inc(free("gT", t), 1)

            def soft(h):
                for i in range(NT):
                    act.wait_ge(max_ready, NT * h + i + 1)
                    act.activation(prob(h, i), prob(h, i), ACT.Exp, bias=nmx(h, i), accum_out=rsum(h, i))\
                        .then_inc(exp_ready, 1)

            soft(0)
            for h in range(H):
                if h + 1 < H:
                    soft(h + 1)
                if h >= 2:
                    multiplied(act, ("pv", h - 2))
                for i in range(NT):
                    o = take(act, "pT", h, i)
                    w = P * (i + 1)
                    act.activation(pT[:, h % 2, 0:i + 1, i * P:(i + 1) * P],
                                   o[:, 0:w].rearrange("p (j q) -> p j q", j=i + 1), ACT.Copy)\
                        .then_inc(free("pT", h, i), 1)
                r0 = DH * (h % 2)
                o = take(act, "pv", h)
                act.activation(yaT[r0:r0 + DH, h // 2, :], o[r0:r0 + DH, :], ACT.Copy).then_inc(free("pv", h), 1)
            for t in range(NT):
                for f in range(2):
                    if (t, f) == (0, 0):
                        multiplied(act, ("pv", H - 1))
                    o = take(act, "mT", t, f)
                    act.activation(quads(mT, t, f), four(o), ACT.Copy, scale=0.5).then_inc(free("mT", t, f), 1)
            for t in range(NT):
                for f in range(2):
                    o = take(act, "y", t, f)
                    if (t, f) == (0, 0):
                        act.wait_ge(p_ready, NT * H)
                    act.activation(nat[:, t, f * HALF:(f + 1) * HALF], o[:, :], ACT.Copy)\
                        .then_inc(free("y", t, f), 1)
                stored(act, ("y", t, 0), ("y", t, 1))
                squares(1, t, nat[:, t, :], junk)
            for t in range(NT):
                act.wait_ge(x_new, t + 1)
                squares(2, t, xr[:, t, :], junk)
            for t in range(NT):
                for f in range(2):
                    o = take(act, "h2T", t, f)
                    act.activation(quads(h2T, t, f), four(o), ACT.Copy).then_inc(free("h2T", t, f), 1)
            for h in range(PH):
                o = take(act, "pq", h)
                act.activation(pqT[:, h, :], o[:, :], ACT.Copy).then_inc(free("pq", h), 1)
            for t in range(NT):
                for q in range(4):
                    o = take(act, "sc", t, q)
                    n = t * PH + 2 * q
                    act.activation(scores[:, n:n + 2, :], o[:, :].rearrange("p (e k) -> p e k", e=2), ACT.Copy)\
                        .then_inc(free("sc", t, q), 1)

            def softmax(n, p):
                act.wait_ge(shift_ready, n + 1)
                act.activation(expd[p], shifted[p], ACT.Exp, accum_out=esum[p]).then_inc(soft_ready, 1)

            softmax(0, 0)
            with act.Fori(0, UNITS // 2) as i:
                for p in range(2):
                    n = i * 2 + p
                    act.wait_ge(dots_ready, n + 1)
                    act.activation(act_out[p], act_in[p], ACT.Gelu_apprx_tanh).then_inc(gelu_ready, 1)
                    softmax(n + 1, 1 - p)
            for t in range(NT):
                act.wait_ge(summed, 1)
                squares(3, t, nat[:, t, :], urows[:, 0, :])

        @block.vector
        def _(dve):
            chain = [0]

            def link(ins):
                chain[0] += 1
                ins.then_inc(dve_chain, 1)
                dve.wait_ge(dve_chain, chain[0])

            dve.wait_ge(cond_exp, 1)
            link(dve.tensor_scalar(scol, ecol, 1.0, None, ALU.add))
            link(dve.reciprocal(scol, scol))
            link(dve.tensor_tensor(scol, scol, ccol, ALU.mult))
            for k in range(KD):
                dve.tensor_copy(cond[:, k, :], scol[:, k:k + 1].to_broadcast([P, P])).then_inc(cond_ready, 1)
            dve.wait_ge(ada_b_in, 16)
            for b in range(N_ADA):
                o = take(dve, "ada", b)
                half = mods[:, b // 2, (b % 2) * HALF:(b % 2 + 1) * HALF]
                dve.tensor_tensor(half, o[:, :], half, ALU.add).then_inc(free("ada", b), 1)
            dve.wait_ge(gains_in, 16)
            stored(dve, *group("ada"))
            for row, gain, one in ((1, 0, 1.0), (2, 1, 0.0), (4, 2, 1.0), (5, 3, 0.0)):
                link(dve.scalar_tensor_tensor(mods[:, row, :], mods[:, row, :], one, gains[:, gain, :],
                                              ALU.add, ALU.mult))
            for t in range(NT):
                dve.wait_ge(rstd_ready, t + 1)
                link(dve.scalar_tensor_tensor(nat[:, t, :], xr[:, t, :], rstd(0, t), mods[:, 1, :],
                                              ALU.mult, ALU.mult))
                dve.tensor_tensor(nat[:, t, :], nat[:, t, :], mods[:, 0, :], ALU.add).then_inc(h_ready, 1)
            for t in range(NT):
                o = take(dve, "in", 2, t)
                dve.tensor_copy(va[:, t, :], o[:, :]).then_inc(free("in", 2, t), 1)
            for t in range(NT):
                stored(dve, ("in", 4, t))
                link(dve.bn_stats(bn(t), zv[:, t, :]))
                dve.bn_aggr(mv(t), bn(t)).then_inc(v_var, 1)
            dve.wait_ge(ln_in, 16)
            dve.wait_ge(v_var, NT)
            for t in range(NT):
                dve.wait_ge(v_rs, t + 1)
                link(dve.tensor_scalar(zv[:, t, :], zv[:, t, :], mv(t)[:, 0:1], v_rstd(t), ALU.subtract, ALU.mult))
                link(dve.tensor_tensor(zv[:, t, :], zv[:, t, :], ln_row[:, 0, :], ALU.mult))
                dve.tensor_tensor(zv[:, t, :], zv[:, t, :], ln_row[:, 1, :], ALU.add).then_inc(v_normed, 1)
            dve.wait_ge(v_normed, NT)
            dve.wait_ge(bs_in, 16)
            stored(dve, *[("in", 3, t) for t in range(NT)])
            for q in range(4):
                o = take(dve, "mix", q)
                for e in range(2):
                    g = 2 * q + e
                    u = zu[:, :, g * GD:(g + 1) * GD]
                    ins = dve.scalar_tensor_tensor(u, o[:, e * 256:(e + 1) * 256].rearrange("p (n c) -> p n c", n=NT),
                                                   bs[:, g:g + 1], u, ALU.add, ALU.mult)
                    ins.then_inc(yg_ready, 1)
                dve.wait_ge(yg_ready, 2 * q + 2)
                dve.nop().then_inc(free("mix", q), 1)

            def biased(h):
                if h >= 2:
                    multiplied(dve, *[("pT", h - 2, i) for i in range(NT)])
                for i in range(NT):
                    o = take(dve, "s", h, i)
                    w = P * (i + 1)
                    link(dve.tensor_tensor_reduce(out=prob(h, i), in0=o[:, 0:w], in1=bias[:, h, S - w:S], scale=1.0,
                                                  scalar=LOWEST, op0=ALU.add, op1=ALU.max, accum_out=mx(h, i)))
                    dve.nop().then_inc(free("s", h, i), 1)
                    dve.tensor_scalar(nmx(h, i), mx(h, i), -1.0, None, ALU.mult).then_inc(max_ready, 1)

            def normed(h):
                for i in range(NT):
                    dve.wait_ge(exp_ready, NT * h + i + 1)
                    link(dve.reciprocal(rinv(h, i), rsum(h, i)))
                    dve.tensor_scalar(prob(h, i), prob(h, i), rinv(h, i), None, ALU.mult).then_inc(p_ready, 1)

            stored(dve, *group("bt"))
            biased(0)
            for h in range(H):
                if h + 1 < H:
                    biased(h + 1)
                normed(h)
            stored(dve, *group("in"))
            for t in range(NT):
                for f in range(2):
                    cut = slice(f * HALF, (f + 1) * HALF)
                    o = take(dve, "ba", t, f)
                    dve.scalar_tensor_tensor(ga[:, t, cut], ga[:, t, cut], 1.0, o[:, :], ALU.add, ALU.mult)\
                        .then_inc(free("ba", t, f), 1)
                    o = take(dve, "bg", t, f)
                    dve.scalar_tensor_tensor(gg[:, t, cut], gg[:, t, cut], 1.0, o[:, :], ALU.add, ALU.mult)\
                        .then_inc(free("bg", t, f), 1)
                    stored(dve, ("ba", t, f), ("bg", t, f))
                    dve.tensor_tensor(ga[:, t, cut], ga[:, t, cut], gg[:, t, cut], ALU.add).then_inc(merged, 1)
            for t in range(NT):
                dve.wait_ge(rstd_ready, NT + t + 1)
                link(dve.scalar_tensor_tensor(nat[:, t, :], nat[:, t, :], rstd(1, t), mods[:, 2, :],
                                              ALU.mult, ALU.mult))
                dve.tensor_tensor(xr[:, t, :], xr[:, t, :], nat[:, t, :], ALU.add).then_inc(x_new, 1)
            multiplied(dve, *group("mT"))
            for t in range(NT):
                dve.wait_ge(rstd_ready, 2 * NT + t + 1)
                link(dve.scalar_tensor_tensor(h2[:, t, :], xr[:, t, :], rstd(2, t), mods[:, 4, :],
                                              ALU.mult, ALU.mult))
                dve.tensor_tensor(h2[:, t, :], h2[:, t, :], mods[:, 3, :], ALU.add).then_inc(h2_ready, 1)
            dve.wait_ge(h2_ready, NT)
            link(dve.tensor_copy(iota_f, iota_i))
            link(dve.memset(nat[:, :, :], 0.0))
            link(dve.memset(scores[:, UNITS, :], 0.0))
            stored(dve, *group("sc"))
            multiplied(dve, *group("pq"))

            base, ticks = [0], [0]

            def tick(ins):
                ticks[0] += 1
                ins.then_inc(dve_tick, 1)
                return ticks[0]

            def after(n):
                dve.wait_ge(dve_tick, base[0] + n)

            def after_apart(n):
                dve.wait_ge(dve_tick, base[0] + n)
                dve.nop().then_inc(dve_passed, 1)

            def top_two_sides(n, p, extra):
                after_apart(tick(dve.tensor_copy(cur, scores_at(n))))
                marks = []
                for a in range(2):
                    marks.append(tick(dve.max(top[:, a, 0:8], cur[:, a, :])))
                for a in range(2):
                    after_apart(marks[a])
                    dve.max_index(top_i[:, a, 0:8], top[:, a, 0:8], cur[:, a, :])
                    marks[a] = tick(dve.match_replace(cur[:, a, :], top[:, a, 0:8], cur[:, a, :], LOWEST))
                for a in range(2):
                    after_apart(marks[a])
                    marks[a] = tick(dve.max(top[:, a, 8:16], cur[:, a, :]))
                for a in range(2):
                    after_apart(marks[a])
                    marks[a] = tick(dve.max_index(top_i[:, a, 8:16], top[:, a, 8:16], cur[:, a, :]))
                c3 = tick(dve.tensor_tensor(cand, top[:, 0, :].unsqueeze(2).to_broadcast([P, TOPK, TOPK]),
                                            top[:, 1, :].unsqueeze(1).to_broadcast([P, TOPK, TOPK]), ALU.add))
                after(marks[1])
                tick(dve.tensor_copy(top_f, top_i))
                after_apart(c3)
                m = tick(dve.max(best[:, 0:8], flat(cand)))
                after_apart(m)
                dve.max_index(best_i[:, 0:8], best[:, 0:8], flat(cand))
                m = tick(dve.match_replace(flat(cand), best[:, 0:8], flat(cand), LOWEST))
                after_apart(m)
                m = tick(dve.max(best[:, 8:16], flat(cand)))
                after_apart(m)
                m = tick(dve.max_index(best_i[:, 8:16], best[:, 8:16], flat(cand)))
                dve.tensor_scalar(shifted[p], best, best[:, 0:1], None, ALU.subtract).then_inc(shift_ready, 1)
                after(m)
                tick(dve.tensor_single_scalar(pair_i[:, 0, :], best_i, 4, ALU.logical_shift_right))
                m = tick(dve.tensor_single_scalar(pair_i[:, 1, :], best_i, 15, ALU.bitwise_and))
                after(m)
                m = tick(dve.tensor_copy(pair_f, flat(pair_i)))
                after(m)
                m = tick(dve.tensor_tensor(match, iota_f.unsqueeze(1).to_broadcast([P, 2 * TOPK, TOPK]),
                                           pair_f.unsqueeze(2).to_broadcast([P, 2 * TOPK, TOPK]), ALU.is_equal))
                after(m)
                m4 = match.rearrange("p (a s) j -> p a s j", a=2)
                for a in range(2):
                    m = tick(dve.tensor_tensor(m4[:, a], m4[:, a],
                                               top_f[:, a, :].unsqueeze(1).to_broadcast([P, TOPK, TOPK]), ALU.mult))
                after(m)
                m = tick(dve.tensor_reduce(key, match, AX, ALU.add))
                after(m)
                dve.scalar_tensor_tensor(idx[p], key[:, 0:TOPK], float(NK), key[:, TOPK:2 * TOPK],
                                         ALU.mult, ALU.add).then_inc(idx_ready, 1)

            def flat(a):
                return a.rearrange("p a b -> p (a b)")

            def scores_at(n):
                if isinstance(n, int):
                    return scores[:, n, :].rearrange("p (a k) -> p a k", a=2)
                return scores[:, bass.ds(n, 1), :].rearrange("p o (a k) -> p (o a) k", a=2)

            def unit(t, n, p):
                for g in range(NGRP):
                    dve.wait_ge(u_in[g], n * (16 * GRP) + 16 * GRP)
                    for s in range(g * GRP, (g + 1) * GRP):
                        ins = dve.scalar_tensor_tensor(urows[:, s, :], urows[:, s, :], 1.0, h2[:, t, :],
                                                       ALU.mult, ALU.mult, accum_out=act_in[p][:, s:s + 1])
                        if s % GRP < GRP - 1:
                            continue
                        ins.then_inc(u_free, 1)
                dve.wait_ge(u_free, n * NGRP + 2 * NGRP)
                dve.nop().then_inc(dots_ready, 1)
                top_two_sides(n + 1, 1 - p, True)
                dve.wait_ge(soft_ready, n + 1)
                dve.wait_ge(gelu_ready, n + 1)
                after(tick(dve.reciprocal(einv[p], esum[p])))
                m = tick(dve.scalar_tensor_tensor(coef[p], act_out[p], einv[p], expd[p], ALU.mult, ALU.mult))
                after(m)
                for g in range(NGRP):
                    dve.wait_ge(v_in[g % 2], n * (32 * GRP) + 16 * GRP * (g // 2 + 1))
                    for s in range(g * GRP, (g + 1) * GRP):
                        ins = dve.scalar_tensor_tensor(nat[:, t, :], vrows[s % 8], coef[p][:, s:s + 1], nat[:, t, :],
                                                       ALU.mult, ALU.add)
                        if s % GRP == GRP - 1:
                            ins.then_inc(v_free, 1)
                            dve.wait_ge(v_free, n * NGRP + (g + 3))
                        else:
                            after(tick(ins))

            top_two_sides(0, 0, False)
            dve.nop().then_inc(u_free, NGRP)
            dve.nop().then_inc(v_free, 2)
            before = ticks[0]
            with dve.Fori(0, NT) as t:
                with dve.Fori(0, PH // 2) as j:
                    for p in range(2):
                        base[0] = t * (PH * UNIT_TICKS) + j * (2 * UNIT_TICKS) + (before + p * UNIT_TICKS)
                        ticks[0] = 0
                        unit(t, t * PH + j * 2 + p, p)
                        assert ticks[0] == UNIT_TICKS, ticks[0]
            dve.nop().then_inc(summed, 1)
            for t in range(NT):
                dve.wait_ge(rstd_ready, 3 * NT + t + 1)
                link(dve.scalar_tensor_tensor(nat[:, t, :], nat[:, t, :], rstd(3, t), mods[:, 5, :],
                                              ALU.mult, ALU.mult))
                dve.tensor_tensor(nat[:, t, :], xr[:, t, :], nat[:, t, :], ALU.add).then_inc(out_ready, 1)


def kernel(x, c, ada_w, ada_b, pre_g1, post_g1, w_in, gmlp_ln_g, gmlp_ln_b, gmlp_w_s, gmlp_b_s, rel_bias,
           w_branch_attn, w_branch_gmlp, w_out, pre_g2, post_g2, peer_w_query, peer_sub_keys, peer_u, peer_v):
    import concourse.bacc as bacc
    from concourse.bass_utils import run_bass_kernel_spmd

    a = np.asarray
    half = QD // 2
    keys = np.zeros((QD, 2 * NK), np.float32)
    for side in range(2):
        keys[side * half:(side + 1) * half, side * NK:(side + 1) * NK] = a(peer_sub_keys)[0, side].T
    arrays = {
        "x": a(x), "c": a(c)[0].reshape(KD, P).T, "ada_w": a(ada_w)[0], "ada_b": a(ada_b)[0],
        "rows_g": np.concatenate([a(pre_g1)[0], a(post_g1)[0], a(pre_g2)[0], a(post_g2)[0]]),
        "w_in": a(w_in)[0], "ln_gb": np.stack([a(gmlp_ln_g)[0], a(gmlp_ln_b)[0]]),
        "w_s": a(gmlp_w_s)[0].transpose(2, 0, 1), "b_s": a(gmlp_b_s)[0].T, "rel": a(rel_bias),
        "w_branch": np.concatenate([a(w_branch_attn)[0], a(w_branch_gmlp)[0]]), "w_out": a(w_out)[0],
        "w_query": a(peer_w_query)[0], "keys": keys, "u_exp": a(peer_u)[0], "v_exp": a(peer_v)[0],
        "hot": bucket_onehot(), "ident_in": np.eye(P, dtype=np.float32),
        "anti_in": np.eye(P, dtype=np.float32)[::-1],
    }
    arrays = {k: np.ascontiguousarray(v) for k, v in arrays.items()}
    nc = bacc.Bacc("TRN2", target_bir_lowering=False, num_devices=1)
    args = [nc.dram_tensor(k, list(v.shape), F32, kind="ExternalInput").ap() for k, v in arrays.items()]
    out = nc.dram_tensor("out", [1, S, D], F32, kind="ExternalOutput").ap()
    build(nc, *args, out)
    return run_bass_kernel_spmd(nc, [arrays], core_ids=[0]).results[0]["out"]
```

```python
from contextlib import ExitStack
import math

import numpy as np

import concourse.bass as bass
from concourse import mybir

P = 128
D = 1024
S = 512
NT = S // P
KD = D // P
HALF = 512
H, DH = 8, 64
AW = H * DH
GW = D // 2
G, GD = 8, 64
BUCKETS, MAX_DIST = 32, 2048
PH, NK, QD = 8, 128, 128
TOPK = 16
EPS = 1e-6
NEG = -1e30
LOWEST = -3.0e38

F32 = mybir.dt.float32
F32R = mybir.dt.float32r
U32 = mybir.dt.uint32
ALU = mybir.AluOpType
ACT = mybir.ActivationFunctionType
AX = mybir.AxisListType.X

N_ADA, N_IN = 6 * D // HALF, (3 * AW + 2 * GW + 2 * D) // HALF
BLK_ADA, BLK_IN = 0, N_ADA
BLK_BRANCH = BLK_IN + N_IN
BLK_OUT = BLK_BRANCH + 2
BLK_QUERY = BLK_OUT + 2
N_BLK = BLK_QUERY
RING = 3
GRP = 4
DT = NT - 1
DS = DT * P
STEP = 4
N_STEP = NK // STEP
HEAD_TICKS = 23


def bucket_onehot():
    n = (S - 1) - np.arange(2 * S)
    exact = BUCKETS // 2
    nf = np.maximum(n, exact).astype(np.float32)
    large = exact + (np.log(nf / np.float32(exact)) / np.float32(math.log(MAX_DIST / exact))
                     * np.float32(BUCKETS - exact)).astype(np.int32)
    b = np.where(n < exact, n, np.minimum(large, BUCKETS - 1))
    hot = (np.arange(BUCKETS)[:, None] == b[None, :]) & (n >= 0)[None, :]
    return np.concatenate([hot, (n < 0)[None, :]]).astype(np.float32)



GATE_BLK = 5


def gate_jobs(a, b):
    return [("in", GATE_BLK + n // 4, n % 4) for n in range(a, b)]


def gates_before(h):
    at = 4 + 2 * h if h < 4 else 8 + h
    return gate_jobs(at, at + 1)


def gates_behind(h):
    return gate_jobs(5 + 2 * h, 6 + 2 * h) if h < 4 else []


JOBS = {}
for _names in (
    [("ext", f) for f in range(2)],
    [("ada", b) for b in range(N_ADA)],
    [("hT", t, f) for t in range(NT) for f in range(2)],
    [("bt", h) for h in range(H)],
    [("in", b, j) for b in range(GATE_BLK) for j in range(4)],
    gate_jobs(0, 2), [("mix", q) for q in range(4)], [("s", 0, i) for i in range(NT)],
    gate_jobs(2, 4), [("gT", t) for t in range(NT)],
    [job for h in range(H) for job in
     [("s", h + 1, i) for i in range(NT) if h + 1 < H] + gates_before(h) + [("pT", h, i) for i in range(NT)]
     + gates_behind(h) + [("pv", h)]],
    [(a, t, f) for t in range(NT) for f in range(2) for a in ("ba", "bg")],
    [("mT", t, f) for t in range(NT) for f in range(2)],
    [("y", t, f) for t in range(2) for f in range(2)],
    [job for t in range(NT) for job in
     [("h2T", t, f) for f in range(2)] + [("pq", t, f) for f in range(2)] + [("sc", t, q) for q in range(4)]
     + [("y", t + 2, f) for f in range(2) if t + 2 < NT]],
    [("kT", t) for t in range(1, NT)],
):
    for _n in _names:
        JOBS[_n] = len(JOBS)


NORMS = [(0, t) for t in range(NT)] + [(1, 0), (1, 1), (2, 0), (2, 1), (1, 2), (1, 3), (2, 2), (2, 3)] \
    + [(3, t) for t in range(NT)]
NORM_NO = {norm: n + 1 for n, norm in enumerate(NORMS)}


def build(nc, x, c, ada_w, ada_b, rows_g, w_in, ln_gb, w_s, b_s, rel, w_branch, w_out, w_query, keys,
  u_exp, u_by_key, v_exp, hot, ident_in, anti_in, out):
    bias_dram = nc.dram_tensor("bias_scratch", [H, 2 * S], F32, kind="Internal").ap()
    ctx = ExitStack()
    with ctx:
        def sb(name, shape, dt=F32):
            return ctx.enter_context(nc.sbuf_tensor(name, shape, dt))

        def sem(name):
            return ctx.enter_context(nc.semaphore(name))

        base_byte = -(-nc.sbuf_base // 64) * 64

        def at(name, kb, shape, dt=F32):
            t = nc.alloc_sbuf_tensor_at(name, shape, dt, offset=base_byte + int(kb * 1024))
            return t[tuple(slice(None) for _ in shape)]

        xr = at("xr", 0, [P, NT, D])
        gate2 = at("gate2", 16, [P, D])
        cond = at("cond", 20, [P, KD, P])
        wsT = at("wsT", 20, [P, G, P])
        probs = at("probs", 24, [P, 2, 1280])
        ln_row = at("ln_row", 24, [P, 2, GW])
        ext = at("ext", 24, [H, 2 * S])
        hot_sb = at("hot_sb", 29, [BUCKETS + 1, 2 * S])
        small = at("small", 34, [P, 256])
        ident = at("ident", 35, [P, P])
        nat = at("nat", 35.5, [P, NT, D])
        bias = at("bias", 35.5, [P, H, S])
        mods5 = at("mods5", 51.5, [P, 5, D])
        ring = at("ring", 71.5, [P, RING, KD, HALF])
        hT = at("hT", 119.5, [P, KD, S])
        pT = at("pT", 0, [P, 2, NT, S])
        mT = at("mT", 119.5, [P, KD, S])
        qT = at("qT", 135.5, [P, NT, S])
        kT = at("kT", 143.5, [P, NT, S])
        anti = at("anti", 143.5, [P, P])
        va = at("va", 151.5, [P, NT, S])
        zu = at("zu", 159.5, [P, NT, S])
        junk = at("junk", 159.5, [P, D])
        zv = at("zv", 167.5, [P, NT, S])
        yaT, ygT = qT, zv
        ga = at("ga", 175.5, [P, NT, D])
        gains = at("gains", 175.5, [P, 4, D])
        gg = at("gg", 191.5, [P, NT, D])
        flipped = at("flipped", 191.5, [P, H, S])

        h2_0 = at("h2_0", 20, [P, D])
        pqT = at("pqT", 24, [P, PH, P])
        acc0 = at("acc0", 28, [P, D])
        skb = at("skb", 32, [P, 2 * NK])
        junk2 = at("junk2", 87.5, [P, D])
        picks = at("picks", 91.5, [P, NT, 3, P])
        h2T = at("h2T", 119.5, [P, KD, S])
        wq = at("wq", 135.5, [P, 2, KD, HALF])
        cur = at("cur", 167.5, [P, 2, NK])
        cand = at("cand", 168.5, [P, TOPK, TOPK])
        match = at("match", 169.5, [P, 2 * TOPK, TOPK])
        spot = at("spot", 171.5, [P, 512])
        h2 = at("h2", 175.5, [P, NT, D])
        scores = at("scores", 191.5, [P, 2, PH, 2 * NK])
        top = spot[:, 0:32].rearrange("p (a k) -> p a k", a=2)
        top_i = spot[:, 32:64].bitcast(U32).rearrange("p (a k) -> p a k", a=2)
        top_f = spot[:, 64:96].rearrange("p (a k) -> p a k", a=2)
        best = spot[:, 96:112]
        best_i = spot[:, 112:128].bitcast(U32)
        pair_i = spot[:, 128:160].bitcast(U32).rearrange("p (a k) -> p a k", a=2)
        pair_f = spot[:, 160:192]
        iota_f = spot[:, 192:208]
        esum, einv = spot[:, 208:216], spot[:, 216:224]
        expd = spot[:, 224:352]
        shifted = spot[:, 352:480]

        split_at = 183.5
        h2_hi = at("h2_hi", split_at, [P, KD, DS], F32R)
        h2_lo = at("h2_lo", split_at + 12, [P, KD, DS], F32R)
        picksT = at("picksT", 175.5, [P, 3, DS])
        idx0 = at("idx0", 180, [P, P], U32)
        gate0 = at("gate0", 180.5, [P, P])
        hot1 = at("hot1", 163.5, [P, 2, 4, P])
        hot2 = at("hot2", 167.5, [P, 2, 4, P])
        lane_i = at("lane_i", 174.5, [P, P], mybir.dt.int32)
        lane = at("lane", 175, [P, P])
        staged = [at("staged0", 35.5, [P, NK, P]), at("staged1", 99.5, [P, NK, P])]

        u_raw = at("u_raw", 35.5, [P, STEP, KD, P])
        v_raw = at("v_raw", 51.5, [P, STEP, D])
        u_hi = at("u_hi", 67.5, [P, 2, KD, P], F32R)
        u_lo = at("u_lo", 75.5, [P, 2, KD, P], F32R)
        v_hi = at("v_hi", 83.5, [P, 2, D], F32R)
        v_lo = at("v_lo", 91.5, [P, 2, D], F32R)
        w_row = at("w_row", 99.5, [P, STEP, DS])
        gel = at("gel", 105.5, [P, 2, DS])
        gated = at("gated", 108.5, [P, 2, DS])
        g_hi = at("g_hi", 111.5, [P, 2, DS], F32R)
        g_lo = at("g_lo", 114.5, [P, 2, DS], F32R)
        u_rows = at("u_rows", 117.5, [P, GRP, D])
        v_rows = at("v_rows", 133.5, [P, GRP, D])
        y_out = at("y_out", 35.5, [P, DT, D])
        junk3 = at("junk3", 51.5, [P, D])
        tiny = at("tiny", 181, [P, 64])
        idx_u, idx_v = tiny[:, 0:4].bitcast(U32), tiny[:, 4:8].bitcast(U32)
        dots, dots_gelu, coef = tiny[:, 8:12], tiny[:, 12:16], tiny[:, 16:20]

        def mod(row):
            return gate2[:, :] if row == 5 else mods5[:, row, :]

        def cols(a, n=1):
            return small[:, a:a + n]

        sumsq, ms, rstd = (lambda k, t: cols(4 * k + t)), (lambda k, t: cols(16 + 4 * k + t)), \
            (lambda k, t: cols(32 + 4 * k + t))
        mhalf = cols(48)
        bs = cols(52, G)
        bn, mv = (lambda t: cols(60 + 6 * t, 6)), (lambda t: cols(84 + 2 * t, 2))
        v_ms, v_rstd = (lambda t: cols(92 + t)), (lambda t: cols(96 + t))
        mx, nmx, rsum, rinv = (lambda h, i: cols(100 + 4 * (h % 4) + i)), (lambda h, i: cols(116 + 4 * (h % 4) + i)), \
            (lambda h, i: cols(132 + 4 * (h % 4) + i)), (lambda h, i: cols(148 + 4 * (h % 4) + i))
        ccol, ecol, scol = cols(164, KD), cols(172, KD), cols(180, KD)
        rel_sb = small[0:BUCKETS + 1, 188:188 + H]
        iota_i = small[:, 200:216].bitcast(mybir.dt.int32)

        def prob(h, i):
            at = [0, 128, 384, 768][i]
            return probs[:, h % 2, at:at + P * (i + 1)]

        banks = [ctx.enter_context(nc.psum_tensor(f"bank{i}", [P, HALF], F32)) for i in range(8)]
        bank_full = [sem(f"bank_full{i}") for i in range(8)]
        bank_free = [sem(f"bank_free{i}") for i in range(8)]

        def bank(*job):
            return banks[JOBS[job] % 8]

        def take(eng, *job):
            eng.wait_ge(bank_full[JOBS[job] % 8], JOBS[job] // 8 + 1)
            return bank(*job)

        def free(*job):
            return bank_free[JOBS[job] % 8]

        def last_of(jobs):
            return {n % 8: n // 8 + 1 for n in sorted(JOBS[job] for job in jobs)}

        def stored(eng, *jobs):
            for b, n in last_of(jobs).items():
                eng.wait_ge(bank_free[b], n)

        def multiplied(eng, *jobs):
            for b, n in last_of(jobs).items():
                eng.wait_ge(bank_full[b], n)

        def group(kind):
            return [j for j in JOBS if j[0] == kind]

        x_in = [sem(f"x_in{t}") for t in range(NT)]
        c_in, ada_b_in, gains_in, ident_landed, ln_in, ws_in, bs_in = (
            sem(n) for n in ("c_in", "ada_b_in", "gains_in", "ident_landed", "ln_in", "ws_in", "bs_in"))
        hot_in, rel_in, rel_mask, bias_out, bias_in, keys_in = (
            sem(n) for n in ("hot_in", "rel_in", "rel_mask", "bias_out", "bias_in", "keys_in"))
        blk_in = [sem(f"blk_in{r}") for r in range(RING)]
        cond_exp, cond_ready, sq_ready, rstd_ready, pool_const, pool_chain, dve_chain = (
            sem(n) for n in ("cond_exp", "cond_ready", "sq_ready", "rstd_ready", "pool_const", "pool_chain",
                             "dve_chain"))
        h_ready, v_var, v_rs, v_normed, ws_masked, yg_ready, max_ready, exp_ready, p_ready = (
            sem(n) for n in ("h_ready", "v_var", "v_rs", "v_normed", "ws_masked", "yg_ready", "max_ready",
                             "exp_ready", "p_ready"))
        merged, x_new, h2_ready, idx_ready, shift_ready, soft_ready, dots_ready, gelu_ready = (
            sem(n) for n in ("merged", "x_new", "h2_ready", "idx_ready", "shift_ready", "soft_ready",
                             "dots_ready", "gelu_ready"))
        wq_in, expd_ready, h2_hi_done, h2_lo_done, picks_ready, hot_ready, hot_used, w_full, w_staged = (
            sem(n) for n in ("wq_in", "expd_ready", "h2_hi_done", "h2_lo_done", "picks_ready", "hot_ready",
                             "hot_used", "w_full", "w_staged"))
        picked, merge_read, own_gelu_done, y_taken = (
            sem(n) for n in ("picked", "merge_read", "own_gelu_done", "y_taken"))
        w_stored = [sem(f"w_stored{i}") for i in range(2)]
        u_raw_in, v_raw_in, w_row_in = ([sem(f"{n}{q}") for q in range(STEP)]
                                        for n in ("u_raw_in", "v_raw_in", "w_row_in"))
        u_hi_done, u_lo_done, v_hi_done, v_lo_done, a_full, gel_done, gated_done, g_hi_done, g_lo_done, v_done = (
            sem(n) for n in ("u_hi_done", "u_lo_done", "v_hi_done", "v_lo_done", "a_full", "gel_done",
                             "gated_done", "g_hi_done", "g_lo_done", "v_done"))
        idx_u_set, idx_v_set, u_rows_in, v_rows_in, u_rows_used, v_rows_used, coef_tick, acc_tick = (
            sem(n) for n in ("idx_u_set", "idx_v_set", "u_rows_in", "v_rows_in", "u_rows_used", "v_rows_used",
                             "coef_tick", "acc_tick"))
        out_ready, out_stored = sem("out_ready"), sem("out_stored")
        dve_tick, dve_passed, pool_passed = sem("dve_tick"), sem("dve_passed"), sem("pool_passed")

        w_dram = nc.dram_tensor("w_scratch", [P, NK, DS], F32, kind="Internal").ap()
        DS_GROUPS = P // 4
        v_rows_by = v_exp.rearrange("(i b) d -> b i d", b=NK)

        def turn(j, q):
            return j // STEP + 1

        class Blocks:
            def __init__(self, array, axis):
                self.array, self.axis = array, axis

            def __getitem__(self, b):
                at_b = slice(b, b + 1) if isinstance(b, int) else bass.ds(b, 1)
                if self.axis == 0:
                    return self.array[at_b].rearrange("o p n -> (o p) n")
                return self.array[:, at_b].rearrange("p o n -> p (o n)")

        u_blocks, v_blocks, w_rows = Blocks(u_by_key, 0), Blocks(v_rows_by, 0), Blocks(w_dram, 1)

        def sp_regions_free(eng):
            eng.wait_ge(w_stored[1], 16)

        def blk(n):
            return ring[:, n % RING]

        w_src = []
        for b in range(N_ADA):
            w_src.append(ada_w[:, b * HALF:(b + 1) * HALF].rearrange("(k p) n -> p k n", p=P))
        for b in range(N_IN):
            w_src.append(w_in[:, b * HALF:(b + 1) * HALF].rearrange("(k p) n -> p k n", p=P))
        for b in range(2):
            w_src.append(w_branch[:, b * HALF:(b + 1) * HALF].rearrange("(k p) n -> p k n", p=P))
        for b in range(2):
            w_src.append(w_out[:, b * HALF:(b + 1) * HALF].rearrange("(k p) n -> p k n", p=P))

        last_reader = [("ada", b) for b in range(N_ADA)] + [("in", b, 3) for b in range(N_IN)] \
            + [("bg", NT - 1, 0), ("bg", NT - 1, 1), ("y", NT - 1, 0), ("y", NT - 1, 1)]

        block = ctx.enter_context(nc.Block())

        @block.sync
        def _(sp):
            sp.dma_start(ccol, c).then_inc(c_in, 16)
            sp.dma_start(hot_sb, hot).then_inc(hot_in, 16)
            sp.wait_ge(rel_mask, 1)
            sp.dma_start(rel_sb[0:BUCKETS, :], rel).then_inc(rel_in, 16)
            for n in range(N_BLK):
                if n >= RING:
                    multiplied(sp, last_reader[n - RING])
                sp.dma_start(blk(n), w_src[n]).then_inc(blk_in[n % RING], 16)
                if n == 1:
                    sp.dma_start(mods5.rearrange("p a d -> p (a d)"),
                                 ada_b[0:5 * D].partition_broadcast(P)).then_inc(ada_b_in, 16)
                    sp.dma_start(gate2, ada_b[5 * D:6 * D].partition_broadcast(P)).then_inc(ada_b_in, 16)
                if n == 2:
                    sp.dma_start(ident[:, :], ident_in).then_inc(ident_landed, 16)
                    sp.dma_start(anti, anti_in).then_inc(ident_landed, 16)
                    sp.dma_start(gains[:, :, :].rearrange("p a d -> p (a d)"),
                                 rows_g.partition_broadcast(P)).then_inc(gains_in, 16)
                    for t in range(NT):
                        sp.dma_start(xr[:, t, :], x[0, t * P:(t + 1) * P, :]).then_inc(x_in[t], 16)
                    sp.dma_start(bs, b_s).then_inc(bs_in, 16)
            multiplied(sp, *group("pv"))
            for t in range(NT):
                sp.dma_start(xr[:, t, :], x[0, t * P:(t + 1) * P, :]).then_inc(x_in[t], 16)
            multiplied(sp, *group("ba"), *group("bg"))
            for b in range(2):
                sp.dma_start(wq[:, b], w_query[:, b * HALF:(b + 1) * HALF].rearrange("(k p) n -> p k n", p=P))\
                    .then_inc(wq_in, 16)
            for t in range(DT):
                sp.wait_ge(w_staged, DS_GROUPS * (t + 1))
                sp.dma_start(w_dram[:, :, t * P:(t + 1) * P], staged[t % 2]).then_inc(w_stored[t % 2], 16)

            def load(q, b):
                sp.dma_start(u_raw[:, q].rearrange("p k e -> p (k e)"), u_blocks[b]).then_inc(u_raw_in[q], 16)
                sp.dma_start(v_raw[:, q], v_blocks[b]).then_inc(v_raw_in[q], 16)
                sp.dma_start(w_row[:, q], w_rows[b]).then_inc(w_row_in[q], 16)

            sp.wait_ge(w_stored[0], 32)
            sp.wait_ge(w_stored[1], 16)
            for q in range(STEP):
                load(q, q)

            def refill(n, q):
                b = n * STEP + q
                sp.wait_ge(u_lo_done, b + 1)
                sp.wait_ge(v_lo_done, b + 1)
                sp.wait_ge(gated_done, b + 1)
                load(q, b + STEP)

            for q in range(STEP):
                refill(0, q)
            with sp.Fori(1, N_STEP - 1) as n:
                for q in range(STEP):
                    refill(n, q)
            for t in range(NT):
                sp.wait_ge(out_ready, t + 1)
                sp.dma_start(out[0, t * P:(t + 1) * P, :], acc0 if t == 0 else y_out[:, t - 1])\
                    .then_inc(out_stored, 16)
            sp.wait_ge(out_stored, 16 * NT)

        @block.gpsimd
        def _(pool):
            chain = [0]

            def link(ins):
                chain[0] += 1
                ins.then_inc(pool_chain, 1)
                pool.wait_ge(pool_chain, chain[0])

            def norm(k, t):
                pool.wait_ge(sq_ready, NORM_NO[k, t])
                link(pool.tensor_scalar(ms(k, t), sumsq(k, t), 1.0 / D, EPS, ALU.mult, ALU.add))
                pool.tensor_tensor(rstd(k, t), ms(k, t), mhalf, ALU.pow).then_inc(rstd_ready, 1)

            pool.memset(rel_sb, NEG).then_inc(rel_mask, 1)
            link(pool.memset(mhalf, -0.5))
            link(pool.iota(iota_i, pattern=[[1, TOPK]], base=0, channel_multiplier=0))
            stored(pool, ("ext", 0), ("ext", 1))
            pool.dma_start(bias_dram, ext).then_inc(bias_out, 16)
            for t in range(NT):
                norm(0, t)
            pool.wait_ge(bias_out, 16)
            pool.dma_start(flipped, bass.AP(bias_dram.tensor, 0, [[1, P], [2 * S, H], [1, S]]))\
                .then_inc(bias_in, 16)
            pool.dma_start(ln_row, ln_gb.partition_broadcast(P)).then_inc(ln_in, 16)
            multiplied(pool, *group("ada"))
            pool.dma_start(wsT[:, :, :], w_s).then_inc(ws_in, 16)
            pool.wait_ge(ws_in, 16)
            pool.affine_select(out=wsT[:, :, :], in_=wsT[:, :, :], compare_op=ALU.is_ge, fill=0.0, base=0,
                               pattern=[[0, G], [1, P]], channel_multiplier=-1).then_inc(ws_masked, 1)
            for t in range(NT):
                pool.wait_ge(v_var, t + 1)
                link(pool.tensor_scalar(v_ms(t), mv(t)[:, 1:2], 1.0, EPS, ALU.mult, ALU.add))
                pool.tensor_tensor(v_rstd(t), v_ms(t), mhalf, ALU.pow).then_inc(v_rs, 1)
            multiplied(pool, *group("ba"))
            pool.dma_start(skb, keys).then_inc(keys_in, 16)
            for k, t in NORMS[NT:3 * NT]:
                norm(k, t)
            link(pool.iota(lane_i, pattern=[[1, P]], base=0, channel_multiplier=0))
            pool.tensor_copy(lane, lane_i).then_inc(pool_const, 1)

            def gather(table, rows, ix, signal):
                for s in range(GRP):
                    pool.indirect_dma_start(out=rows[:, s], out_offset=None, in_=table,
                                            in_offset=bass.IndirectOffsetOnAxis(ap=ix[:, s:s + 1], axis=0))\
                        .then_inc(signal, 16)

            def group_of(n):
                return idx0[:, n * GRP:(n + 1) * GRP] if isinstance(n, int) else idx0[:, bass.ds(n * GRP, GRP)]

            multiplied(pool, *group("h2T"))
            pool.wait_ge(idx_ready, 1)
            sp_regions_free(pool)
            pool.tensor_copy(idx_u, group_of(0)).then_inc(idx_u_set, 1)
            pool.wait_ge(idx_u_set, 1)
            gather(u_exp, u_rows, idx_u, u_rows_in)
            pool.tensor_copy(idx_v, group_of(0)).then_inc(idx_v_set, 1)
            pool.wait_ge(idx_v_set, 1)
            gather(v_exp, v_rows, idx_v, v_rows_in)

            def next_rows(n):
                pool.wait_ge(u_rows_used, n + 1)
                pool.nop().then_inc(pool_passed, 1)
                pool.tensor_copy(idx_u, group_of(n + 1)).then_inc(idx_u_set, 1)
                pool.wait_ge(idx_u_set, n + 2)
                pool.nop().then_inc(pool_passed, 1)
                gather(u_exp, u_rows, idx_u, u_rows_in)
                pool.wait_ge(v_rows_used, n + 1)
                pool.nop().then_inc(pool_passed, 1)
                pool.tensor_copy(idx_v, group_of(n + 1)).then_inc(idx_v_set, 1)
                pool.wait_ge(idx_v_set, n + 2)
                pool.nop().then_inc(pool_passed, 1)
                gather(v_exp, v_rows, idx_v, v_rows_in)

            with pool.Fori(0, N_STEP - 1) as n:
                next_rows(n)
            for t in range(NT):
                norm(3, t)

        @block.tensor
        def _(pe):
            def start(*job):
                if JOBS[job] >= 8:
                    pe.wait_ge(free(*job), JOBS[job] // 8)
                return bank(*job)

            def full(last, *job):
                last.then_inc(bank_full[JOBS[job] % 8], 1)

            def arrived(n):
                pe.wait_ge(blk_in[n % RING], 16 * (n // RING + 1))
                return blk(n)

            def product(job, pairs):
                o = start(*job)
                for k, (a, b) in enumerate(pairs):
                    last = pe.matmul(o[:, :], a, b, start=(k == 0), stop=(k == len(pairs) - 1))
                full(last, *job)

            def transposes(job, blocks):
                o = start(*job)
                for k, a in enumerate(blocks):
                    last = pe.transpose(o[:, k * P:(k + 1) * P], a, ident[:, :])
                full(last, *job)

            pe.wait_ge(hot_in, 16)
            pe.wait_ge(rel_in, 16)
            for f in range(2):
                o = start("ext", f)
                full(pe.matmul(o[0:H, :], rel_sb, hot_sb[:, f * HALF:(f + 1) * HALF], start=True, stop=True),
                     "ext", f)
            pe.wait_ge(cond_ready, KD)
            for b in range(N_ADA):
                w = arrived(BLK_ADA + b)
                product(("ada", b), [(cond[:, k, :], w[:, k, :]) for k in range(KD)])
            pe.wait_ge(ident_landed, 32)
            for t in range(NT):
                pe.wait_ge(h_ready, t + 1)
                for f in range(2):
                    transposes(("hT", t, f), [nat[:, t, (4 * f + k) * P:(4 * f + k + 1) * P] for k in range(4)])
            pe.wait_ge(bias_in, 16)
            pe.wait_ge(ident_landed, 32)
            for h in range(H):
                product(("bt", h), [(anti, flipped[:, h, :])])
            stored(pe, *group("hT"))
            def project(*jobs):
                for _, b, j in jobs:
                    w = arrived(BLK_IN + b)
                    cut = slice(j * P, (j + 1) * P)
                    product(("in", b, j), [(w[:, k, cut], hT[:, k, :]) if b < 2 else (hT[:, k, cut], w[:, k, :])
                                           for k in range(KD)])

            def logits(h):
                r0 = DH * (h % 2)
                for i in range(NT):
                    o = start("s", h, i)
                    w = P * (i + 1)
                    full(pe.matmul(o[:, 0:w], qT[r0:r0 + DH, h // 2, i * P:(i + 1) * P],
                                   kT[r0:r0 + DH, h // 2, 0:w], start=True, stop=True), "s", h, i)

            project(*[("in", b, j) for b in range(GATE_BLK) for j in range(4)])
            project(*gate_jobs(0, 2))
            pe.wait_ge(ws_masked, 1)
            pe.wait_ge(v_normed, NT)
            for q in range(4):
                o = start("mix", q)
                for e in range(2):
                    g = 2 * q + e
                    last = pe.matmul(o[:, e * 256:(e + 1) * 256], wsT[:, g, :], zv[:, :, g * GD:(g + 1) * GD],
                                     start=True, stop=True)
                full(last, "mix", q)
            stored(pe, *[("in", b, j) for b in range(3) for j in range(4)])
            logits(0)
            project(*gate_jobs(2, 4))
            pe.wait_ge(yg_ready, G)
            for t in range(NT):
                transposes(("gT", t), [zu[:, t, k * P:(k + 1) * P] for k in range(4)])
            for h in range(H):
                if h + 1 < H:
                    logits(h + 1)
                project(*gates_before(h))
                for i in range(NT):
                    pe.wait_ge(p_ready, NT * h + i + 1)
                    transposes(("pT", h, i), [prob(h, i)[:, j * P:(j + 1) * P] for j in range(i + 1)])
                project(*gates_behind(h))
                stored(pe, *[("pT", h, i) for i in range(NT)])
                o = start("pv", h)
                r0 = DH * (h % 2)
                for j in range(NT):
                    last = pe.matmul(o[r0:r0 + DH, j * P:S], va[:, j, h * DH:(h + 1) * DH],
                                     pT[:, h % 2, j, j * P:S], start=(j == 0), stop=(j == NT - 1))
                full(last, "pv", h)
            stored(pe, *group("pv"), *group("gT"))
            wb = [arrived(BLK_BRANCH), arrived(BLK_BRANCH + 1)]
            for t in range(NT):
                cut = slice(t * P, (t + 1) * P)
                for f in range(2):
                    product(("ba", t, f), [(yaT[:, k, cut], wb[f][:, k, :]) for k in range(4)])
                    product(("bg", t, f), [(ygT[:, k, cut], wb[f][:, 4 + k, :]) for k in range(4)])
            for t in range(NT):
                for f in range(2):
                    pe.wait_ge(merged, 2 * t + f + 1)
                    transposes(("mT", t, f), [ga[:, t, (4 * f + k) * P:(4 * f + k + 1) * P] for k in range(4)])
            wo = [arrived(BLK_OUT), arrived(BLK_OUT + 1)]
            def mixer_out(t):
                stored(pe, ("mT", t, 0), ("mT", t, 1))
                for f in range(2):
                    product(("y", t, f), [(mT[:, k, t * P:(t + 1) * P], wo[f][:, k, :]) for k in range(KD)])

            mixer_out(0)
            mixer_out(1)
            pe.wait_ge(wq_in, 32)
            pe.wait_ge(keys_in, 16)
            for t in range(NT):
                cut = slice(t * P, (t + 1) * P)
                pe.wait_ge(h2_ready, t + 1)
                for f in range(2):
                    rows = h2_0 if t == 0 else h2[:, t]
                    transposes(("h2T", t, f), [rows[:, (4 * f + k) * P:(4 * f + k + 1) * P] for k in range(4)])
                stored(pe, ("h2T", t, 0), ("h2T", t, 1))
                for f in range(2):
                    o = start("pq", t, f)
                    for j in range(4):
                        for k in range(KD):
                            last = pe.matmul(o[:, j * P:(j + 1) * P], wq[:, f, k, j * P:(j + 1) * P], h2T[:, k, cut],
                                             start=(k == 0), stop=(k == KD - 1))
                    full(last, "pq", t, f)
                stored(pe, ("pq", t, 0), ("pq", t, 1))
                for q in range(4):
                    o = start("sc", t, q)
                    for e in range(2):
                        last = pe.matmul(o[:, e * 256:(e + 1) * 256], pqT[:, 2 * q + e, :], skb,
                                         start=True, stop=True)
                    full(last, "sc", t, q)
                if t + 2 < NT:
                    mixer_out(t + 2)

            for t in range(1, NT):
                pe.wait_ge(picks_ready, t + 1)
                transposes(("kT", t), [picks[:, t, a, :] for a in range(3)])
            stored(pe, *[j for j in JOBS if JOBS[j] >= len(JOBS) - 8])

            def spread(g, r):
                pe.wait_ge(hot_ready, g + 1)
                if isinstance(g, int):
                    if g >= 2:
                        pe.wait_ge(w_staged, g - 1)
                else:
                    pe.wait_ge(w_staged, g - 1)
                for j in range(4):
                    last = pe.matmul(banks[6 + r][:, j * P:(j + 1) * P], hot1[:, r, j], hot2[:, r, j],
                                     start=True, stop=True)
                last.then_inc(w_full, 1)

            for g in range(2):
                spread(g, g)
            with pe.Fori(1, DT * DS_GROUPS // 2) as m:
                for r in range(2):
                    spread(m * 2 + r, r)

            def first(j, r):
                pe.wait_ge(u_lo_done, j + 1)
                if not isinstance(j, int) or j >= 2:
                    pe.wait_ge(gel_done, j - 1)
                o = banks[6 + r][:, 0:DS]
                for k in range(KD):
                    pe.matmul(o, u_hi[:, r, k], h2_hi[:, k], start=(k == 0), stop=False)
                    pe.matmul(o, u_hi[:, r, k], h2_lo[:, k], start=False, stop=False)
                    last = pe.matmul(o, u_lo[:, r, k], h2_hi[:, k], start=False, stop=(k == KD - 1))
                last.then_inc(a_full, 1)

            def second(j, r):
                pe.wait_ge(v_lo_done, j + 1)
                pe.wait_ge(g_lo_done, j + 1)
                is_first, is_last = (isinstance(j, int) and j == n for n in (0, NK - 1))
                for t in range(DT):
                    cut = slice(t * P, (t + 1) * P)
                    for f in range(2):
                        o, half = banks[2 * t + f][:, :], slice(f * HALF, (f + 1) * HALF)
                        pe.matmul(o, g_hi[:, r, cut], v_hi[:, r, half], start=is_first, stop=False)
                        pe.matmul(o, g_hi[:, r, cut], v_lo[:, r, half], start=False, stop=False)
                        last = pe.matmul(o, g_lo[:, r, cut], v_hi[:, r, half], start=False, stop=is_last)
                last.then_inc(v_done, 1)

            pe.wait_ge(w_staged, DT * DS_GROUPS)
            pe.wait_ge(h2_lo_done, 1)
            first(0, 0)
            for q in range(STEP):
                first(q + 1, (q + 1) % 2)
                second(q, q % 2)
            with pe.Fori(1, N_STEP - 1) as n:
                for q in range(STEP):
                    first(n * STEP + (q + 1), (q + 1) % 2)
                    second(n * STEP + q, q % 2)
            for b in range(NK - STEP, NK):
                if b + 1 < NK:
                    first(b + 1, (b + 1) % 2)
                second(b, b % 2)

        @block.scalar
        def _(act):
            def quads(a, t, f):
                return a[:, 4 * f:4 * f + 4, t * P:(t + 1) * P]

            def four(o):
                return o[:, :].rearrange("p (k t) -> p k t", k=4)

            def squares(k, t, a, spare):
                if NT * k + t:
                    act.wait_ge(sq_ready, NT * k + t)
                act.activation(spare, a, ACT.Square, accum_out=sumsq(k, t)).then_inc(sq_ready, 1)

            act.wait_ge(c_in, 16)
            act.activation(ecol, ccol, ACT.Exp, scale=-1.0).then_inc(cond_exp, 1)
            for f in range(2):
                o = take(act, "ext", f)
                act.activation(ext[:, f * HALF:(f + 1) * HALF], o[0:H, :], ACT.Copy).then_inc(free("ext", f), 1)
            for t in range(NT):
                act.wait_ge(x_in[t], 16)
                squares(0, t, xr[:, t, :], junk)
            for t in range(NT):
                for f in range(2):
                    o = take(act, "hT", t, f)
                    act.activation(quads(hT, t, f), four(o), ACT.Copy).then_inc(free("hT", t, f), 1)
            for h in range(H):
                o = take(act, "bt", h)
                act.activation(bias[:, h, :], o[:, :], ACT.Copy).then_inc(free("bt", h), 1)
            act.wait_ge(sq_ready, NT)
            for b in range(GATE_BLK):
                if b == 2:
                    continue
                for j in range(4):
                    o = take(act, "in", b, j)
                    done = free("in", b, j)
                    if b == 0:
                        act.activation(qT[:, j, :], o[:, :], ACT.Copy, scale=DH ** -0.5).then_inc(done, 1)
                    elif b == 1:
                        act.activation(kT[:, j, :], o[:, :], ACT.Copy).then_inc(done, 1)
                    else:
                        act.activation((zu, zv)[b - 3][:, j, :], o[:, :], ACT.Gelu_apprx_tanh).then_inc(done, 1)

            def gates(jobs):
                for _, b, j in jobs:
                    o = take(act, "in", b, j)
                    gate, f = (ga, b - 5) if b < 7 else (gg, b - 7)
                    act.activation(gate[:, j, f * HALF:(f + 1) * HALF], o[:, :], ACT.Tanh, scale=0.5)\
                        .then_inc(free("in", b, j), 1)

            def soft(h):
                for i in range(NT):
                    act.wait_ge(max_ready, NT * h + i + 1)
                    act.activation(prob(h, i), prob(h, i), ACT.Exp, bias=nmx(h, i), accum_out=rsum(h, i))\
                        .then_inc(exp_ready, 1)

            act.wait_ge(h_ready, NT)
            gates(gate_jobs(0, 4))
            soft(0)
            multiplied(act, *group("mix"))
            for t in range(NT):
                o = take(act, "gT", t)
                act.activation(ygT[:, :, t * P:(t + 1) * P], four(o), ACT.Copy).then_inc(free("gT", t), 1)
            for h in range(H):
                if h + 1 < H:
                    soft(h + 1)
                gates(gates_before(h))
                if h >= 2:
                    multiplied(act, ("pv", h - 2))
                for i in range(NT):
                    o = take(act, "pT", h, i)
                    w = P * (i + 1)
                    act.activation(pT[:, h % 2, 0:i + 1, i * P:(i + 1) * P],
                                   o[:, 0:w].rearrange("p (j q) -> p j q", j=i + 1), ACT.Copy)\
                        .then_inc(free("pT", h, i), 1)
                gates(gates_behind(h))
                r0 = DH * (h % 2)
                o = take(act, "pv", h)
                act.activation(yaT[r0:r0 + DH, h // 2, :], o[r0:r0 + DH, :], ACT.Copy).then_inc(free("pv", h), 1)
            for t in range(NT):
                for f in range(2):
                    if (t, f) == (0, 0):
                        multiplied(act, ("pv", H - 1))
                    o = take(act, "mT", t, f)
                    act.activation(quads(mT, t, f), four(o), ACT.Copy, scale=0.5).then_inc(free("mT", t, f), 1)
            def mixer_out(t):
                for f in range(2):
                    o = take(act, "y", t, f)
                    act.activation(nat[:, t, f * HALF:(f + 1) * HALF], o[:, :], ACT.Copy)\
                        .then_inc(free("y", t, f), 1)
                stored(act, ("y", t, 0), ("y", t, 1))

            sq = [NT]

            def squares_of(k, t, a, spare):
                act.wait_ge(sq_ready, sq[0])
                act.activation(spare, a, ACT.Square, accum_out=sumsq(k, t)).then_inc(sq_ready, 1)
                sq[0] += 1

            def x_squares(t):
                act.wait_ge(x_new, t + 1)
                squares_of(2, t, xr[:, t, :], junk2)

            act.wait_ge(p_ready, NT * H)
            multiplied(act, *group("ba"), *group("bg"))
            mixer_out(0)
            squares_of(1, 0, nat[:, 0, :], junk2)
            mixer_out(1)
            squares_of(1, 1, nat[:, 1, :], junk2)
            x_squares(0)
            x_squares(1)
            for t in range(NT):
                for f in range(2):
                    o = take(act, "h2T", t, f)
                    act.activation(quads(h2T, t, f), four(o), ACT.Copy).then_inc(free("h2T", t, f), 1)
                if t:
                    multiplied(act, *[("sc", t - 1, q) for q in range(4)])
                for f in range(2):
                    o = take(act, "pq", t, f)
                    act.activation(pqT[:, 4 * f:4 * f + 4, :], four(o), ACT.Copy).then_inc(free("pq", t, f), 1)
                if t >= 2:
                    act.wait_ge(picked, t - 1)
                else:
                    act.wait_ge(merge_read, 1)
                for q in range(4):
                    o = take(act, "sc", t, q)
                    act.activation(scores[:, t % 2, 2 * q:2 * q + 2, :], o[:, :].rearrange("p (e k) -> p e k", e=2),
                                   ACT.Copy).then_inc(free("sc", t, q), 1)
                if t + 2 < NT:
                    mixer_out(t + 2)
                    squares_of(1, t + 2, nat[:, t + 2, :], junk2)
                if t:
                    act.wait_ge(picked, t)
                    act.activation(expd, shifted, ACT.Exp).then_inc(expd_ready, 1)
                if 2 <= t + 1 < NT:
                    x_squares(t + 1)
            act.wait_ge(picked, NT)
            act.activation(expd, shifted, ACT.Exp).then_inc(expd_ready, 1)
            act.wait_ge(picks_ready, NT)
            act.activation(h2_hi, h2T[:, :, P:S], ACT.Copy).then_inc(h2_hi_done, 1)
            for t in range(1, NT):
                o = take(act, "kT", t)
                act.activation(picksT[:, :, (t - 1) * P:t * P], o[:, 0:3 * P].rearrange("p (a t) -> p a t", a=3),
                               ACT.Copy).then_inc(free("kT", t), 1)

            def stage(g, r, t, at_token):
                act.wait_ge(w_full, g + 1)
                o = banks[6 + r][:, :].rearrange("p (t b) -> p b t", t=4)
                tokens = slice(at_token, at_token + 4) if isinstance(at_token, int) else bass.ds(at_token, 4)
                act.activation(staged[t % 2][:, :, tokens], o, ACT.Copy).then_inc(w_staged, 1)

            for t in range(DT):
                if t == 0:
                    multiplied(act, *group("kT"))
                if t == 1:
                    act.wait_ge(h2_lo_done, 1)
                if t == 2:
                    act.wait_ge(w_stored[0], 16)
                with act.Fori(0, DS_GROUPS // 2) as m:
                    for r in range(2):
                        stage(m * 2 + (t * DS_GROUPS + r), r, t, m * 8 + 4 * r)

            def u_high(j, q):
                r = q % 2
                act.wait_ge(u_raw_in[q], 16 * turn(j, q))
                if not isinstance(j, int) or j >= 2:
                    act.wait_ge(a_full, j - 1)
                act.activation(u_hi[:, r], u_raw[:, q], ACT.Copy).then_inc(u_hi_done, 1)

            def v_high(j, q):
                r = q % 2
                act.wait_ge(v_raw_in[q], 16 * turn(j, q))
                if not isinstance(j, int) or j >= 2:
                    act.wait_ge(v_done, j - 1)
                act.activation(v_hi[:, r], v_raw[:, q], ACT.Copy).then_inc(v_hi_done, 1)

            def block_step(b, q):
                r = q % 2
                act.wait_ge(a_full, b + 1)
                if not isinstance(b, int) or b >= 2:
                    act.wait_ge(gated_done, b - 1)
                act.activation(gel[:, r], banks[6 + r][:, 0:DS], ACT.Gelu_apprx_tanh).then_inc(gel_done, 1)
                if not isinstance(b, int) or b + 2 < NK:
                    u_high(b + 2, (q + 2) % STEP)
                act.wait_ge(gated_done, b + 1)
                if not isinstance(b, int) or b >= 2:
                    act.wait_ge(v_done, b - 1)
                act.activation(g_hi[:, r], gated[:, r], ACT.Copy).then_inc(g_hi_done, 1)
                if not isinstance(b, int) or b + 1 < NK:
                    v_high(b + 1, (q + 1) % STEP)

            def own_gelu(n):
                act.wait_ge(u_rows_used, n + 1)
                act.activation(dots_gelu, dots, ACT.Gelu_apprx_tanh).then_inc(own_gelu_done, 1)

            u_high(0, 0)
            u_high(1, 1)
            v_high(0, 0)
            for q in range(STEP):
                block_step(q, q)
                if q == 1:
                    own_gelu(0)
            with act.Fori(1, N_STEP - 1) as n:
                for q in range(STEP):
                    block_step(n * STEP + q, q)
                    if q == 1:
                        own_gelu(n)
            for q in range(STEP):
                block_step(NK - STEP + q, q)
                if q == 1:
                    own_gelu(N_STEP - 1)
            act.wait_ge(v_done, NK)
            for t in range(DT):
                for f in range(2):
                    act.activation(y_out[:, t, f * HALF:(f + 1) * HALF], banks[2 * t + f][:, :], ACT.Copy)\
                        .then_inc(y_taken, 1)
            act.wait_ge(v_rows_used, N_STEP)
            squares_of(3, 0, acc0, junk3)
            for t in range(1, NT):
                act.wait_ge(y_taken, 2 * t)
                squares_of(3, t, y_out[:, t - 1], junk3)

        @block.vector
        def _(dve):
            chain = [0]

            def link(ins):
                chain[0] += 1
                ins.then_inc(dve_chain, 1)
                dve.wait_ge(dve_chain, chain[0])

            dve.wait_ge(cond_exp, 1)
            link(dve.tensor_scalar(scol, ecol, 1.0, None, ALU.add))
            link(dve.reciprocal(scol, scol))
            link(dve.tensor_tensor(scol, scol, ccol, ALU.mult))
            for k in range(KD):
                dve.tensor_copy(cond[:, k, :], scol[:, k:k + 1].to_broadcast([P, P])).then_inc(cond_ready, 1)
            dve.wait_ge(ada_b_in, 32)
            for b in range(N_ADA):
                o = take(dve, "ada", b)
                half = mod(b // 2)[:, (b % 2) * HALF:(b % 2 + 1) * HALF]
                dve.tensor_tensor(half, o[:, :], half, ALU.add).then_inc(free("ada", b), 1)
            dve.wait_ge(gains_in, 16)
            stored(dve, *group("ada"))
            for row, gain, one in ((1, 0, 1.0), (2, 1, 0.0), (4, 2, 1.0), (5, 3, 0.0)):
                link(dve.scalar_tensor_tensor(mod(row), mod(row), one, gains[:, gain, :],
                                              ALU.add, ALU.mult))
            for t in range(NT):
                dve.wait_ge(rstd_ready, t + 1)
                link(dve.scalar_tensor_tensor(nat[:, t, :], xr[:, t, :], rstd(0, t), mod(1),
                                              ALU.mult, ALU.mult))
                dve.tensor_tensor(nat[:, t, :], nat[:, t, :], mod(0), ALU.add).then_inc(h_ready, 1)
            for t in range(NT):
                o = take(dve, "in", 2, t)
                dve.tensor_copy(va[:, t, :], o[:, :]).then_inc(free("in", 2, t), 1)
            for t in range(NT):
                stored(dve, ("in", 4, t))
                link(dve.bn_stats(bn(t), zv[:, t, :]))
                dve.bn_aggr(mv(t), bn(t)).then_inc(v_var, 1)
            dve.wait_ge(ln_in, 16)
            dve.wait_ge(v_var, NT)
            for t in range(NT):
                dve.wait_ge(v_rs, t + 1)
                link(dve.tensor_scalar(zv[:, t, :], zv[:, t, :], mv(t)[:, 0:1], v_rstd(t), ALU.subtract, ALU.mult))
                link(dve.tensor_tensor(zv[:, t, :], zv[:, t, :], ln_row[:, 0, :], ALU.mult))
                dve.tensor_tensor(zv[:, t, :], zv[:, t, :], ln_row[:, 1, :], ALU.add).then_inc(v_normed, 1)
            dve.wait_ge(v_normed, NT)
            dve.wait_ge(bs_in, 16)
            stored(dve, *[("in", 3, t) for t in range(NT)])
            for q in range(4):
                o = take(dve, "mix", q)
                for e in range(2):
                    g = 2 * q + e
                    u = zu[:, :, g * GD:(g + 1) * GD]
                    ins = dve.scalar_tensor_tensor(u, o[:, e * 256:(e + 1) * 256].rearrange("p (n c) -> p n c", n=NT),
                                                   bs[:, g:g + 1], u, ALU.add, ALU.mult)
                    ins.then_inc(yg_ready, 1)
                dve.wait_ge(yg_ready, 2 * q + 2)
                dve.nop().then_inc(free("mix", q), 1)

            def biased(h):
                if h >= 2:
                    multiplied(dve, *[("pT", h - 2, i) for i in range(NT)])
                for i in range(NT):
                    o = take(dve, "s", h, i)
                    w = P * (i + 1)
                    link(dve.tensor_tensor_reduce(out=prob(h, i), in0=o[:, 0:w], in1=bias[:, h, S - w:S], scale=1.0,
                                                  scalar=LOWEST, op0=ALU.add, op1=ALU.max, accum_out=mx(h, i)))
                    dve.nop().then_inc(free("s", h, i), 1)
                    dve.tensor_scalar(nmx(h, i), mx(h, i), -1.0, None, ALU.mult).then_inc(max_ready, 1)

            def normed(h):
                for i in range(NT):
                    dve.wait_ge(exp_ready, NT * h + i + 1)
                    link(dve.reciprocal(rinv(h, i), rsum(h, i)))
                    dve.tensor_scalar(prob(h, i), prob(h, i), rinv(h, i), None, ALU.mult).then_inc(p_ready, 1)

            stored(dve, *group("bt"))
            biased(0)
            for h in range(H):
                if h + 1 < H:
                    biased(h + 1)
                normed(h)
            stored(dve, *group("in"))
            for t in range(NT):
                for f in range(2):
                    cut = slice(f * HALF, (f + 1) * HALF)
                    o = take(dve, "ba", t, f)
                    dve.scalar_tensor_tensor(ga[:, t, cut], ga[:, t, cut], 1.0, o[:, :], ALU.add, ALU.mult)\
                        .then_inc(free("ba", t, f), 1)
                    o = take(dve, "bg", t, f)
                    dve.scalar_tensor_tensor(gg[:, t, cut], gg[:, t, cut], 1.0, o[:, :], ALU.add, ALU.mult)\
                        .then_inc(free("bg", t, f), 1)
                    stored(dve, ("ba", t, f), ("bg", t, f))
                    dve.tensor_tensor(ga[:, t, cut], ga[:, t, cut], gg[:, t, cut], ALU.add).then_inc(merged, 1)
            dve.nop().then_inc(merge_read, 1)

            def x_step(t):
                dve.wait_ge(rstd_ready, NORM_NO[1, t])
                dve.wait_ge(x_in[t], 32)
                link(dve.scalar_tensor_tensor(nat[:, t, :], nat[:, t, :], rstd(1, t), mod(2), ALU.mult, ALU.mult))
                dve.tensor_tensor(xr[:, t, :], xr[:, t, :], nat[:, t, :], ALU.add).then_inc(x_new, 1)

            def h2_step(t):
                rows = h2_0 if t == 0 else h2[:, t]
                dve.wait_ge(rstd_ready, NORM_NO[2, t])
                link(dve.scalar_tensor_tensor(rows, xr[:, t, :], rstd(2, t), mod(4), ALU.mult, ALU.mult))
                dve.tensor_tensor(rows, rows, mod(3), ALU.add).then_inc(h2_ready, 1)

            base, ticks = [0], [0]

            def tick(ins):
                ticks[0] += 1
                ins.then_inc(dve_tick, 1)
                return ticks[0]

            def after(n):
                dve.wait_ge(dve_tick, base[0] + n)

            def after_apart(n):
                dve.wait_ge(dve_tick, base[0] + n)
                dve.nop().then_inc(dve_passed, 1)

            def top_two_sides(t, h):
                places = bass.ds(h * TOPK, TOPK)
                source = scores[:, t % 2, bass.ds(h, 1), :].rearrange("p o (a k) -> p (o a) k", a=2)
                after_apart(tick(dve.tensor_copy(cur, source)))
                marks = []
                for a in range(2):
                    marks.append(tick(dve.max(top[:, a, 0:8], cur[:, a, :])))
                for a in range(2):
                    after_apart(marks[a])
                    dve.max_index(top_i[:, a, 0:8], top[:, a, 0:8], cur[:, a, :])
                    marks[a] = tick(dve.match_replace(cur[:, a, :], top[:, a, 0:8], cur[:, a, :], LOWEST))
                for a in range(2):
                    after_apart(marks[a])
                    marks[a] = tick(dve.max(top[:, a, 8:16], cur[:, a, :]))
                for a in range(2):
                    after_apart(marks[a])
                    marks[a] = tick(dve.max_index(top_i[:, a, 8:16], top[:, a, 8:16], cur[:, a, :]))
                c3 = tick(dve.tensor_tensor(cand, top[:, 0, :].unsqueeze(2).to_broadcast([P, TOPK, TOPK]),
                                            top[:, 1, :].unsqueeze(1).to_broadcast([P, TOPK, TOPK]), ALU.add))
                after(marks[1])
                tick(dve.tensor_copy(top_f, top_i))
                after_apart(c3)
                m = tick(dve.max(best[:, 0:8], flat(cand)))
                after_apart(m)
                dve.max_index(best_i[:, 0:8], best[:, 0:8], flat(cand))
                m = tick(dve.match_replace(flat(cand), best[:, 0:8], flat(cand), LOWEST))
                after_apart(m)
                m = tick(dve.max(best[:, 8:16], flat(cand)))
                after_apart(m)
                m = tick(dve.max_index(best_i[:, 8:16], best[:, 8:16], flat(cand)))
                tick(dve.tensor_scalar(shifted[:, places], best, best[:, 0:1], None, ALU.subtract))
                after(m)
                tick(dve.tensor_single_scalar(pair_i[:, 0, :], best_i, 4, ALU.logical_shift_right))
                m = tick(dve.tensor_single_scalar(pair_i[:, 1, :], best_i, 15, ALU.bitwise_and))
                after(m)
                m = tick(dve.tensor_copy(pair_f, flat(pair_i)))
                after(m)
                m = tick(dve.tensor_tensor(match, iota_f.unsqueeze(1).to_broadcast([P, 2 * TOPK, TOPK]),
                                           pair_f.unsqueeze(2).to_broadcast([P, 2 * TOPK, TOPK]), ALU.is_equal))
                after(m)
                m4 = match.rearrange("p (a s) j -> p a s j", a=2)
                for a in range(2):
                    m = tick(dve.tensor_tensor(m4[:, a], m4[:, a],
                                               top_f[:, a, :].unsqueeze(1).to_broadcast([P, TOPK, TOPK]), ALU.mult))
                after(m)
                tick(dve.tensor_reduce(picks[:, t, 0:2, places], m4, AX, ALU.add))

            def flat(a):
                return a.rearrange("p a b -> p (a b)")

            def pick(t):
                stored(dve, *[("sc", t, q) for q in range(4)])
                start = base[0] + ticks[0]
                with dve.Fori(0, PH) as h:
                    base[0], ticks[0] = h * HEAD_TICKS + start, 0
                    top_two_sides(t, h)
                    assert ticks[0] == HEAD_TICKS, ticks[0]
                base[0], ticks[0] = start + PH * HEAD_TICKS, 0
                after(0)
                dve.nop().then_inc(picked, 1)
                dve.wait_ge(expd_ready, t + 1)
                heads = expd.rearrange("p (h k) -> p h k", h=PH)
                after(tick(dve.tensor_reduce(esum, heads, AX, ALU.add)))
                after(tick(dve.reciprocal(einv, esum)))
                dve.tensor_tensor(picks[:, t, 2, :].rearrange("p (h k) -> p h k", h=PH), heads,
                                  einv.unsqueeze(2).to_broadcast([P, PH, TOPK]), ALU.mult).then_inc(picks_ready, 1)

            x_step(0)
            x_step(1)
            h2_step(0)
            h2_step(1)
            multiplied(dve, *group("mT"))
            dve.wait_ge(h2_ready, 2)
            link(dve.tensor_copy(iota_f, iota_i))
            link(dve.memset(acc0, 0.0))
            pick(0)
            for t in range(2, NT):
                x_step(t)
                h2_step(t)
                pick(t - 1)
            pick(NT - 1)
            dve.wait_ge(picks_ready, NT)
            multiplied(dve, *group("h2T"))
            dve.scalar_tensor_tensor(idx0, picks[:, 0, 0, :], float(NK), picks[:, 0, 1, :], ALU.mult, ALU.add)\
                .then_inc(idx_ready, 1)
            dve.tensor_copy(gate0, picks[:, 0, 2, :]).then_inc(idx_ready, 1)
            dve.wait_ge(idx_ready, 2)
            dve.wait_ge(h2_hi_done, 1)
            dve.tensor_tensor(h2_lo, h2T[:, :, P:S], h2_hi.bitcast(F32), ALU.subtract).then_inc(h2_lo_done, 1)

            stored(dve, *group("kT"))
            multiplied(dve, *group("pq"))
            dve.wait_ge(pool_const, 1)

            def hots(g, r, token):
                if not isinstance(g, int) or g >= 2:
                    dve.wait_ge(w_full, g - 1)
                four = slice(token, token + 4) if isinstance(token, int) else bass.ds(token, 4)
                dve.tensor_tensor(hot1[:, r], lane.unsqueeze(1).to_broadcast([P, 4, P]),
                                  picksT[:, 0, four].unsqueeze(2).to_broadcast([P, 4, P]), ALU.is_equal)
                for j in range(4):
                    at_t = slice(token + j, token + j + 1) if isinstance(token, int) else bass.ds(token + j, 1)
                    ins = dve.tensor_scalar(hot2[:, r, j], lane, picksT[:, 1, at_t], picksT[:, 2, at_t],
                                            ALU.is_equal, ALU.mult)
                ins.then_inc(hot_ready, 1)

            for g in range(2):
                hots(g, g, 4 * g)
            with dve.Fori(1, DT * DS_GROUPS // 2) as m:
                for r in range(2):
                    hots(m * 2 + r, r, m * 8 + 4 * r)

            def u_low(j, q):
                r = q % 2
                dve.wait_ge(u_hi_done, j + 1)
                dve.tensor_tensor(u_lo[:, r], u_raw[:, q], u_hi[:, r].bitcast(F32), ALU.subtract)\
                    .then_inc(u_lo_done, 1)

            def v_low(j, q):
                r = q % 2
                dve.wait_ge(v_hi_done, j + 1)
                dve.tensor_tensor(v_lo[:, r], v_raw[:, q], v_hi[:, r].bitcast(F32), ALU.subtract)\
                    .then_inc(v_lo_done, 1)

            def block_step(b, q):
                r = q % 2
                dve.wait_ge(gel_done, b + 1)
                dve.wait_ge(w_row_in[q], 16 * turn(b, q))
                dve.tensor_tensor(gated[:, r], gel[:, r], w_row[:, q], ALU.mult).then_inc(gated_done, 1)
                if not isinstance(b, int) or b + 2 < NK:
                    u_low(b + 2, (q + 2) % STEP)
                dve.wait_ge(g_hi_done, b + 1)
                dve.tensor_tensor(g_lo[:, r], gated[:, r], g_hi[:, r].bitcast(F32), ALU.subtract)\
                    .then_inc(g_lo_done, 1)
                if not isinstance(b, int) or b + 1 < NK:
                    v_low(b + 1, (q + 1) % STEP)

            def own(n, q):
                if q == 0:
                    dve.wait_ge(u_rows_in, n * (16 * GRP) + 16 * GRP)
                if q < 2:
                    for s in (2 * q, 2 * q + 1):
                        ins = dve.scalar_tensor_tensor(u_rows[:, s], u_rows[:, s], 1.0, h2_0, ALU.mult, ALU.mult,
                                                       accum_out=dots[:, s:s + 1])
                    if q == 1:
                        ins.then_inc(u_rows_used, 1)
                    return
                if q == 2:
                    dve.wait_ge(own_gelu_done, n + 1)
                    dve.wait_ge(v_rows_in, n * (16 * GRP) + 16 * GRP)
                    gates = gate0[:, n * GRP:(n + 1) * GRP] if isinstance(n, int) else gate0[:, bass.ds(n * GRP, GRP)]
                    dve.tensor_tensor(coef, dots_gelu, gates, ALU.mult).then_inc(coef_tick, 1)
                    dve.wait_ge(coef_tick, n + 1)
                for s in (2 * q - 4, 2 * q - 3):
                    ins = dve.scalar_tensor_tensor(acc0, v_rows[:, s], coef[:, s:s + 1], acc0, ALU.mult, ALU.add)
                    if s < GRP - 1:
                        ins.then_inc(acc_tick, 1)
                        dve.wait_ge(acc_tick, n * (GRP - 1) + (s + 1))
                    else:
                        ins.then_inc(v_rows_used, 1)
                        dve.wait_ge(v_rows_used, n + 1)

            u_low(0, 0)
            u_low(1, 1)
            v_low(0, 0)
            for q in range(STEP):
                block_step(q, q)
                own(0, q)
            with dve.Fori(1, N_STEP - 1) as n:
                for q in range(STEP):
                    block_step(n * STEP + q, q)
                    own(n, q)
            for q in range(STEP):
                block_step(NK - STEP + q, q)
                own(N_STEP - 1, q)
            for t in range(NT):
                rows = acc0 if t == 0 else y_out[:, t - 1]
                dve.wait_ge(rstd_ready, NORM_NO[3, t])
                link(dve.scalar_tensor_tensor(rows, rows, rstd(3, t), gate2, ALU.mult, ALU.mult))
                dve.tensor_tensor(rows, xr[:, t, :], rows, ALU.add).then_inc(out_ready, 1)


def kernel(x, c, ada_w, ada_b, pre_g1, post_g1, w_in, gmlp_ln_g, gmlp_ln_b, gmlp_w_s, gmlp_b_s, rel_bias,
           w_branch_attn, w_branch_gmlp, w_out, pre_g2, post_g2, peer_w_query, peer_sub_keys, peer_u, peer_v):
    import concourse.bacc as bacc
    from concourse.bass_utils import run_bass_kernel_spmd

    a = np.asarray
    half = QD // 2
    keys = np.zeros((QD, 2 * NK), np.float32)
    for side in range(2):
        keys[side * half:(side + 1) * half, side * NK:(side + 1) * NK] = a(peer_sub_keys)[0, side].T
    arrays = {
        "x": a(x), "c": a(c)[0].reshape(KD, P).T, "ada_w": a(ada_w)[0], "ada_b": a(ada_b)[0],
        "rows_g": np.concatenate([a(pre_g1)[0], a(post_g1)[0], a(pre_g2)[0], a(post_g2)[0]]),
        "w_in": a(w_in)[0], "ln_gb": np.stack([a(gmlp_ln_g)[0], a(gmlp_ln_b)[0]]),
        "w_s": a(gmlp_w_s)[0].transpose(2, 0, 1), "b_s": a(gmlp_b_s)[0].T, "rel": a(rel_bias),
        "w_branch": np.concatenate([a(w_branch_attn)[0], a(w_branch_gmlp)[0]]), "w_out": a(w_out)[0],
        "w_query": a(peer_w_query)[0], "keys": keys, "u_exp": a(peer_u)[0], 
        "u_by_key": a(peer_u)[0].reshape(NK, NK, KD, P).transpose(1, 3, 2, 0).reshape(NK, P, KD * NK),
        "v_exp": a(peer_v)[0],
        "hot": bucket_onehot(), "ident_in": np.eye(P, dtype=np.float32),
        "anti_in": np.eye(P, dtype=np.float32)[::-1],
    }
    arrays = {k: np.ascontiguousarray(v) for k, v in arrays.items()}
    nc = bacc.Bacc("TRN2", target_bir_lowering=False, num_devices=1)
    args = [nc.dram_tensor(k, list(v.shape), F32, kind="ExternalInput").ap() for k, v in arrays.items()]
    out = nc.dram_tensor("out", [1, S, D], F32, kind="ExternalOutput").ap()
    build(nc, *args, out)
    return run_bass_kernel_spmd(nc, [arrays], core_ids=[0]).results[0]["out"]
```

```python
from contextlib import ExitStack
import math

import numpy as np

import concourse.bass as bass
from concourse import mybir

P = 128
D = 1024
S = 512
NT = S // P
KD = D // P
HALF = 512
H, DH = 8, 64
AW = H * DH
GW = D // 2
G, GD = 8, 64
BUCKETS, MAX_DIST = 32, 2048
PH, NK, QD = 8, 128, 128
TOPK = 16
EPS = 1e-6
NEG = -1e30
LOWEST = -3.0e38

F32 = mybir.dt.float32
F32R = mybir.dt.float32r
U32 = mybir.dt.uint32
ALU = mybir.AluOpType
ACT = mybir.ActivationFunctionType
AX = mybir.AxisListType.X

N_ADA, N_IN = 6 * D // HALF, (3 * AW + 2 * GW + 2 * D) // HALF
ADA_FIRST = 4
BLOCKS = [("ada", b) for b in range(ADA_FIRST)]
for _b in range(N_IN):
    BLOCKS += [("in", _b)] + [("ada", b) for b in (ADA_FIRST + 2 * _b, ADA_FIRST + 2 * _b + 1) if b < N_ADA]
BLOCKS += [(kind, b) for kind in ("branch", "out") for b in range(2)]
BLOCK_NO = {block: n for n, block in enumerate(BLOCKS)}
N_BLK = len(BLOCKS)
RING = 3
GRP = 4
DT = NT - 1
DS = DT * P
STEP = 4
N_STEP = NK // STEP
CORNER = 4
CANDS = CORNER * TOPK + (TOPK - CORNER) * CORNER
HEADS_TICKS = 50
EARLY = 20
POOL_ROWS = 2


def bucket_onehot():
    n = (S - 1) - np.arange(2 * S)
    exact = BUCKETS // 2
    nf = np.maximum(n, exact).astype(np.float32)
    large = exact + (np.log(nf / np.float32(exact)) / np.float32(math.log(MAX_DIST / exact))
                     * np.float32(BUCKETS - exact)).astype(np.int32)
    b = np.where(n < exact, n, np.minimum(large, BUCKETS - 1))
    hot = (np.arange(BUCKETS)[:, None] == b[None, :]) & (n >= 0)[None, :]
    return np.concatenate([hot, (n < 0)[None, :]]).astype(np.float32)


GATE_BLK = 5


def gate_jobs(a, b):
    return [("in", GATE_BLK + n // 4, n % 4) for n in range(a, b)]


def gates_before(h):
    at = 4 + 2 * h if h < 4 else 8 + h
    return gate_jobs(at, at + 1)


def gates_behind(h):
    return gate_jobs(5 + 2 * h, 6 + 2 * h) if h < 4 else []


JOBS = {}
for _names in (
    [("ext", f) for f in range(2)],
    [("ada", b) for b in range(ADA_FIRST)],
    [("hT", t, f) for t in range(NT) for f in range(2)],
    [("bt", h) for h in range(H)],
    [job for kind, b in BLOCKS[ADA_FIRST:BLOCK_NO["in", GATE_BLK]] for job in
     ([("in", b, j) for j in range(4)] if kind == "in" else [("ada", b)])],
    gate_jobs(0, 2), [("mix", q) for q in range(4)], [("s", 0, i) for i in range(NT)],
    gate_jobs(2, 4), [("gT", t) for t in range(NT)],
    [job for h in range(H) for job in
     [("s", h + 1, i) for i in range(NT) if h + 1 < H] + gates_before(h) + [("pT", h, i) for i in range(NT)]
     + gates_behind(h) + [("pv", h)]],
    [(a, t, f) for t in range(NT) for f in range(2) for a in ("ba", "bg")],
    [("mT", t, f) for t in range(NT) for f in range(2)],
    [("y", t, f) for t in range(2) for f in range(2)],
    [job for t in range(NT) for job in
     [("h2T", t, f) for f in range(2)] + [("pq", t, f) for f in range(2)] + [("sc", t, q) for q in range(4)]
     + [("y", t + 2, f) for f in range(2) if t + 2 < NT]],
    [("kT", t) for t in range(1, NT)],
):
    for _n in _names:
        JOBS[_n] = len(JOBS)


NORMS = [(0, t) for t in range(NT)] + [(1, 0), (1, 1), (2, 0), (2, 1), (1, 2), (1, 3), (2, 2), (2, 3)] \
    + [(3, t) for t in range(NT)]
NORM_NO = {norm: n + 1 for n, norm in enumerate(NORMS)}


def build(nc, x, c, ada_w, ada_b, rows_g, w_in, ln_gb, w_s, b_s, rel, w_branch, w_out, w_query, keys,
  u_exp, u_by_key, v_exp, hot, ident_in, anti_in, out):
    bias_dram = nc.dram_tensor("bias_scratch", [H, 2 * S], F32, kind="Internal").ap()
    ctx = ExitStack()
    with ctx:
        def sb(name, shape, dt=F32):
            return ctx.enter_context(nc.sbuf_tensor(name, shape, dt))

        def sem(name):
            return ctx.enter_context(nc.semaphore(name))

        base_byte = -(-nc.sbuf_base // 64) * 64

        def at(name, kb, shape, dt=F32):
            t = nc.alloc_sbuf_tensor_at(name, shape, dt, offset=base_byte + int(kb * 1024))
            return t[tuple(slice(None) for _ in shape)]

        xr = at("xr", 0, [P, NT, D])
        gate2 = at("gate2", 16, [P, D])
        cond = at("cond", 20, [P, KD, P])
        wsT = at("wsT", 20, [P, G, P])
        probs = at("probs", 24, [P, 2, 1280])
        ln_row = at("ln_row", 24, [P, 2, GW])
        ext = at("ext", 24, [H, 2 * S])
        hot_sb = at("hot_sb", 29, [BUCKETS + 1, 2 * S])
        small = at("small", 34, [P, 256])
        ident = at("ident", 35, [P, P])
        nat = at("nat", 35.5, [P, NT, D])
        bias = at("bias", 35.5, [P, H, S])
        mods5 = at("mods5", 51.5, [P, 5, D])
        ring = at("ring", 71.5, [P, RING, KD, HALF])
        hT = at("hT", 119.5, [P, KD, S])
        pT = at("pT", 0, [P, 2, NT, S])
        mT = at("mT", 119.5, [P, KD, S])
        qT = at("qT", 135.5, [P, NT, S])
        kT = at("kT", 143.5, [P, NT, S])
        anti = at("anti", 143.5, [P, P])
        va = at("va", 151.5, [P, NT, S])
        zu = at("zu", 159.5, [P, NT, S])
        junk = at("junk", 159.5, [P, D])
        zv = at("zv", 167.5, [P, NT, S])
        yaT, ygT = qT, zv
        ga = at("ga", 175.5, [P, NT, D])
        gains = at("gains", 175.5, [P, 4, D])
        gg = at("gg", 191.5, [P, NT, D])
        flipped = at("flipped", 191.5, [P, H, S])

        h2_0 = at("h2_0", 20, [P, D])
        pqT = at("pqT", 24, [P, PH, P])
        acc0 = at("acc0", 28, [P, D])
        skb = at("skb", 32, [P, 2 * NK])
        junk2 = at("junk2", 87.5, [P, D])
        picks = [at(f"picks{t}", kb, [P, 3, P]) for t, kb in enumerate((175.5, 99.5, 101, 177))]
        h2T = at("h2T", 119.5, [P, KD, S])
        wq = at("wq", 135.5, [P, 2, KD, HALF])
        cur, cand, match = ([at(f"{name}{e}", kb + off, shape) for e, kb in enumerate((167.5, 28))]
                            for name, off, shape in (("cur", 0, [P, 2, NK]), ("cand", 1, [P, CANDS]),
                                                     ("match", 2, [P, 2 * TOPK, TOPK])))
        spots = [at(f"spot{e}", kb, [P, cols]) for e, (kb, cols) in enumerate(((171.5, 512), (102.5, 256)))]
        h2 = at("h2", 175.5, [P, NT, D])
        scores = at("scores", 191.5, [P, 2, PH, 2 * NK])
        def parts(lo, n, dt=F32):
            return [a[:, lo:lo + n].bitcast(dt) if dt != F32 else a[:, lo:lo + n] for a in spots]

        def halves(views):
            return [v.rearrange("p (a k) -> p a k", a=2) for v in views]

        top = halves(parts(0, 32))
        top_i, top_f = halves(parts(32, 32, U32)), halves(parts(64, 32))
        best = parts(96, TOPK)
        place_i, place_f = parts(112, 3 * TOPK, U32), parts(160, 3 * TOPK)
        pair_f = parts(208, 2 * TOPK)
        corner = parts(240, TOPK)
        iota_f = small[:, 224:240]
        esum, einv = small[:, 240:248], small[:, 248:256]
        expd = [spots[0][:, P * r:P * (r + 1)] for r in (2, 3)]
        shifted = at("shifted", 173.5, [P, 2, P])

        split_at = 183.5
        h2_hi = at("h2_hi", split_at, [P, KD, DS], F32R)
        h2_lo = at("h2_lo", split_at + 12, [P, KD, DS], F32R)
        picksT = at("picksT", 178.5, [P, 3, DS])
        idx0 = at("idx0", 183, [P, P], U32)
        gate0 = picks[0][:, 2, :]
        apart = at("apart", 32, [P, 4, P])
        hot1 = [at(f"hot1_{r}", kb, [P, 4, P]) for r, kb in enumerate((163.5, 165.5, 167.5, 169.5))]
        hot2 = [at(f"hot2_{r}", kb, [P, 4, P]) for r, kb in enumerate((24, 26, 171.5, 32))]
        lane_i = at("lane_i", 174.5, [P, P], mybir.dt.int32)
        lane = at("lane", 175, [P, P])
        staged = [at("staged0", 35.5, [P, NK, P]), at("staged1", 99.5, [P, NK, P])]

        u_raw = at("u_raw", 99.5, [P, STEP, KD, P])
        v_raw = at("v_raw", 115.5, [P, STEP, D])
        w_row = at("w_row", 131.5, [P, STEP, DS])
        u_hi = at("u_hi", 137.5, [P, 2, KD, P], F32R)
        u_lo = at("u_lo", 145.5, [P, 2, KD, P], F32R)
        v_hi = at("v_hi", 153.5, [P, 2, D], F32R)
        v_lo = at("v_lo", 161.5, [P, 2, D], F32R)
        gel = at("gel", 169.5, [P, 2, DS])
        gated = at("gated", 172.5, [P, 2, DS])
        g_hi = at("g_hi", 177, [P, 2, DS], F32R)
        g_lo = at("g_lo", 180, [P, 2, DS], F32R)
        u_rows = at("u_rows", 35.5, [P, GRP, D])
        v_rows = at("v_rows", 51.5, [P, GRP, D])
        y_out = at("y_out", 99.5, [P, DT, D])
        junk3 = at("junk3", 115.5, [P, D])
        tiny = small[:, 224:256]
        idx_u, idx_v = tiny[:, 0:4].bitcast(U32), tiny[:, 4:8].bitcast(U32)
        dots, dots_gelu, coef = tiny[:, 8:12], tiny[:, 12:16], tiny[:, 16:20]

        def mod(row):
            return gate2[:, :] if row == 5 else mods5[:, row, :]

        def cols(a, n=1):
            return small[:, a:a + n]

        sumsq, ms, rstd = (lambda k, t: cols(4 * k + t)), (lambda k, t: cols(16 + 4 * k + t)), \
            (lambda k, t: cols(32 + 4 * k + t))
        mhalf = cols(48)
        one = cols(49)
        four_picks = small[:, 216:224].rearrange("p (a j) -> p a j", a=2)
        bs = cols(52, G)
        bn, mv = (lambda t: cols(60 + 6 * t, 6)), (lambda t: cols(84 + 2 * t, 2))
        v_ms, v_rstd = (lambda t: cols(92 + t)), (lambda t: cols(96 + t))
        mx, nmx, rsum, rinv = (lambda h, i: cols(100 + 4 * (h % 4) + i)), (lambda h, i: cols(116 + 4 * (h % 4) + i)), \
            (lambda h, i: cols(132 + 4 * (h % 4) + i)), (lambda h, i: cols(148 + 4 * (h % 4) + i))
        ccol, ecol, scol = cols(164, KD), cols(172, KD), cols(180, KD)
        rel_sb = small[0:BUCKETS + 1, 188:188 + H]
        iota_i = small[:, 200:216].bitcast(mybir.dt.int32)

        def prob(h, i):
            at = [0, 128, 384, 768][i]
            return probs[:, h % 2, at:at + P * (i + 1)]

        banks = [ctx.enter_context(nc.psum_tensor(f"bank{i}", [P, HALF], F32)) for i in range(8)]
        bank_full = [sem(f"bank_full{i}") for i in range(8)]
        bank_free = [sem(f"bank_free{i}") for i in range(8)]

        def bank(*job):
            return banks[JOBS[job] % 8]

        def take(eng, *job):
            eng.wait_ge(bank_full[JOBS[job] % 8], JOBS[job] // 8 + 1)
            return bank(*job)

        def free(*job):
            return bank_free[JOBS[job] % 8]

        def last_of(jobs):
            return {n % 8: n // 8 + 1 for n in sorted(JOBS[job] for job in jobs)}

        def stored(eng, *jobs):
            for b, n in last_of(jobs).items():
                eng.wait_ge(bank_free[b], n)

        def multiplied(eng, *jobs):
            for b, n in last_of(jobs).items():
                eng.wait_ge(bank_full[b], n)

        def group(kind):
            return [j for j in JOBS if j[0] == kind]

        x_in = [sem(f"x_in{t}") for t in range(NT)]
        c_in, ada_b_in, gains_in, ident_landed, ln_in, ws_in, bs_in = (
            sem(n) for n in ("c_in", "ada_b_in", "gains_in", "ident_landed", "ln_in", "ws_in", "bs_in"))
        hot_in, rel_in, rel_mask, bias_out, bias_in, keys_in = (
            sem(n) for n in ("hot_in", "rel_in", "rel_mask", "bias_out", "bias_in", "keys_in"))
        blk_in = [sem(f"blk_in{r}") for r in range(RING)]
        cond_exp, cond_ready, sq_ready, rstd_ready, pool_const, pool_chain, dve_chain = (
            sem(n) for n in ("cond_exp", "cond_ready", "sq_ready", "rstd_ready", "pool_const", "pool_chain",
                             "dve_chain"))
        h_ready, v_var, v_rs, v_normed, ws_masked, yg_ready, max_ready, exp_ready, p_ready = (
            sem(n) for n in ("h_ready", "v_var", "v_rs", "v_normed", "ws_masked", "yg_ready", "max_ready",
                             "exp_ready", "p_ready"))
        merged, x_new, h2_ready, idx_ready = (sem(n) for n in ("merged", "x_new", "h2_ready", "idx_ready"))
        wq_in, expd_ready, h2_hi_done, h2_lo_done, picks_ready, hot1_act, hot2_pool, hots_dve, apart_done = (
            sem(n) for n in ("wq_in", "expd_ready", "h2_hi_done", "h2_lo_done", "picks_ready", "hot1_act",
                             "hot2_pool", "hots_dve", "apart_done"))
        w_full, w_staged, picks_copied = sem("w_full"), sem("w_staged"), sem("picks_copied")
        picked, merge_read, own_gelu_done, y_taken = (
            sem(n) for n in ("picked", "merge_read", "own_gelu_done", "y_taken"))
        w_stored = [sem(f"w_stored{i}") for i in range(2)]
        u_raw_in, v_raw_in, w_row_in = ([sem(f"{n}{q}") for q in range(STEP)]
                                        for n in ("u_raw_in", "v_raw_in", "w_row_in"))
        u_hi_done, u_lo_done, v_hi_done, v_lo_done, a_full, gel_done, gated_done, g_hi_done, g_lo_done, v_done = (
            sem(n) for n in ("u_hi_done", "u_lo_done", "v_hi_done", "v_lo_done", "a_full", "gel_done",
                             "gated_done", "g_hi_done", "g_lo_done", "v_done"))
        idx_u_set, idx_v_set, u_rows_in, v_rows_in, u_rows_used, v_rows_used, coef_tick, acc_tick = (
            sem(n) for n in ("idx_u_set", "idx_v_set", "u_rows_in", "v_rows_in", "u_rows_used", "v_rows_used",
                             "coef_tick", "acc_tick"))
        chunks_summed, mods_ready = sem("chunks_summed"), sem("mods_ready")
        out_ready, out_stored = sem("out_ready"), sem("out_stored")
        dve_tick, dve_passed, pool_passed = sem("dve_tick"), sem("dve_passed"), sem("pool_passed")

        w_dram = nc.dram_tensor("w_scratch", [P, NK, DS], F32, kind="Internal").ap()
        DS_GROUPS = P // 4
        v_rows_by = v_exp.rearrange("(i b) d -> b i d", b=NK)

        def turn(j, q):
            return j // STEP + 1

        class Blocks:
            def __init__(self, array, axis):
                self.array, self.axis = array, axis

            def __getitem__(self, b):
                at_b = slice(b, b + 1) if isinstance(b, int) else bass.ds(b, 1)
                if self.axis == 0:
                    return self.array[at_b].rearrange("o p n -> (o p) n")
                return self.array[:, at_b].rearrange("p o n -> p (o n)")

        u_blocks, v_blocks, w_rows = Blocks(u_by_key, 0), Blocks(v_rows_by, 0), Blocks(w_dram, 1)

        def blk(n):
            return ring[:, n % RING]

        def landed(eng, *block):
            n = BLOCK_NO[block]
            eng.wait_ge(blk_in[n % RING], 16 * (n // RING + 1))
            return blk(n)

        sources = {"ada": ada_w, "in": w_in, "branch": w_branch, "out": w_out}
        w_src = [sources[kind][:, b * HALF:(b + 1) * HALF].rearrange("(k p) n -> p k n", p=P) for kind, b in BLOCKS]

        def last_reader(n):
            kind, b = BLOCKS[n]
            return {"ada": ("ada", b), "in": ("in", b, 3), "branch": ("bg", NT - 1, b), "out": ("y", NT - 1, b)}[kind]

        block = ctx.enter_context(nc.Block())

        @block.sync
        def _(sp):
            sp.dma_start(ccol, c).then_inc(c_in, 16)
            sp.dma_start(hot_sb, hot).then_inc(hot_in, 16)
            sp.wait_ge(rel_mask, 1)
            sp.dma_start(rel_sb[0:BUCKETS, :], rel).then_inc(rel_in, 16)
            for n in range(N_BLK):
                if n >= RING:
                    multiplied(sp, last_reader(n - RING))
                sp.dma_start(blk(n), w_src[n]).then_inc(blk_in[n % RING], 16)
                if n == 1:
                    sp.dma_start(mods5.rearrange("p a d -> p (a d)"),
                                 ada_b[0:5 * D].partition_broadcast(P)).then_inc(ada_b_in, 16)
                    sp.dma_start(gate2, ada_b[5 * D:6 * D].partition_broadcast(P)).then_inc(ada_b_in, 16)
                if n == 2:
                    sp.dma_start(ident[:, :], ident_in).then_inc(ident_landed, 16)
                    sp.dma_start(anti, anti_in).then_inc(ident_landed, 16)
                    sp.dma_start(gains[:, :, :].rearrange("p a d -> p (a d)"),
                                 rows_g.partition_broadcast(P)).then_inc(gains_in, 16)
                    for t in range(NT):
                        sp.dma_start(xr[:, t, :], x[0, t * P:(t + 1) * P, :]).then_inc(x_in[t], 16)
                    sp.dma_start(bs, b_s).then_inc(bs_in, 16)
            multiplied(sp, *group("pv"))
            for t in range(NT):
                sp.dma_start(xr[:, t, :], x[0, t * P:(t + 1) * P, :]).then_inc(x_in[t], 16)
            multiplied(sp, *group("ba"), *group("bg"))
            for b in range(2):
                sp.dma_start(wq[:, b], w_query[:, b * HALF:(b + 1) * HALF].rearrange("(k p) n -> p k n", p=P))\
                    .then_inc(wq_in, 16)
            def load_experts(q, b):
                sp.dma_start(u_raw[:, q].rearrange("p k e -> p (k e)"), u_blocks[b]).then_inc(u_raw_in[q], 16)
                sp.dma_start(v_raw[:, q], v_blocks[b]).then_inc(v_raw_in[q], 16)

            def load_gates(q, b):
                sp.dma_start(w_row[:, q], w_rows[b]).then_inc(w_row_in[q], 16)

            def store_gates(t, lo, hi, signal):
                sp.wait_ge(w_staged, DS_GROUPS * (t + 1))
                sp.dma_start(w_dram[:, lo:hi, t * P:(t + 1) * P], staged[t % 2][:, lo:hi]).then_inc(signal, 16)

            store_gates(0, 0, NK, w_stored[0])
            store_gates(1, 0, NK, w_stored[1])
            sp.wait_ge(w_stored[1], 16)
            for q in range(STEP):
                load_experts(q, q)
            sp.wait_ge(w_stored[0], 16)
            store_gates(2, 0, 2 * STEP, w_stored[1])
            sp.wait_ge(w_stored[1], 32)
            for q in range(STEP):
                load_gates(q, q)
            store_gates(2, 2 * STEP, NK, w_stored[0])

            def refill(n, q):
                b = n * STEP + q
                sp.wait_ge(u_lo_done, b + 1)
                sp.wait_ge(v_lo_done, b + 1)
                sp.wait_ge(gated_done, b + 1)
                load_experts(q, b + STEP)
                load_gates(q, b + STEP)

            for q in range(STEP):
                refill(0, q)
            sp.wait_ge(w_stored[0], 32)
            with sp.Fori(1, N_STEP - 1) as n:
                for q in range(STEP):
                    refill(n, q)
            for t in range(NT):
                sp.wait_ge(out_ready, t + 1)
                sp.dma_start(out[0, t * P:(t + 1) * P, :], acc0 if t == 0 else y_out[:, t - 1])\
                    .then_inc(out_stored, 16)
            sp.wait_ge(out_stored, 16 * NT)

        @block.gpsimd
        def _(pool):
            chain = [0]

            def link(ins):
                chain[0] += 1
                ins.then_inc(pool_chain, 1)
                pool.wait_ge(pool_chain, chain[0])

            def norm(k, t):
                pool.wait_ge(sq_ready, NORM_NO[k, t])
                link(pool.tensor_scalar(ms(k, t), sumsq(k, t), 1.0 / D, EPS, ALU.mult, ALU.add))
                pool.tensor_tensor(rstd(k, t), ms(k, t), mhalf, ALU.pow).then_inc(rstd_ready, 1)

            pool.memset(rel_sb, NEG).then_inc(rel_mask, 1)
            link(pool.memset(mhalf, -0.5))
            link(pool.iota(iota_i, pattern=[[1, TOPK]], base=0, channel_multiplier=0))
            stored(pool, ("ext", 0), ("ext", 1))
            pool.dma_start(bias_dram, ext).then_inc(bias_out, 16)
            for t in range(NT):
                norm(0, t)
            pool.wait_ge(bias_out, 16)
            pool.dma_start(flipped, bass.AP(bias_dram.tensor, 0, [[1, P], [2 * S, H], [1, S]]))\
                .then_inc(bias_in, 16)
            pool.dma_start(ln_row, ln_gb.partition_broadcast(P)).then_inc(ln_in, 16)
            multiplied(pool, *group("ada"))
            pool.dma_start(wsT[:, :, :], w_s).then_inc(ws_in, 16)
            pool.wait_ge(ws_in, 16)
            pool.affine_select(out=wsT[:, :, :], in_=wsT[:, :, :], compare_op=ALU.is_ge, fill=0.0, base=0,
                               pattern=[[0, G], [1, P]], channel_multiplier=-1).then_inc(ws_masked, 1)
            for t in range(NT):
                pool.wait_ge(v_var, t + 1)
                link(pool.tensor_scalar(v_ms(t), mv(t)[:, 1:2], 1.0, EPS, ALU.mult, ALU.add))
                pool.tensor_tensor(v_rstd(t), v_ms(t), mhalf, ALU.pow).then_inc(v_rs, 1)
            multiplied(pool, *group("ba"))
            pool.dma_start(skb, keys).then_inc(keys_in, 16)
            for k, t in NORMS[NT:3 * NT]:
                norm(k, t)
            pool.memset(one, 1.0).then_inc(pool_const, 1)
            link(pool.iota(lane_i, pattern=[[1, P]], base=0, channel_multiplier=0))
            pool.tensor_copy(lane, lane_i).then_inc(pool_const, 1)

            def gather(table, rows, ix, signal):
                for s in range(GRP):
                    pool.indirect_dma_start(out=rows[:, s], out_offset=None, in_=table,
                                            in_offset=bass.IndirectOffsetOnAxis(ap=ix[:, s:s + 1], axis=0))\
                        .then_inc(signal, 16)

            def group_of(n):
                return idx0[:, n * GRP:(n + 1) * GRP] if isinstance(n, int) else idx0[:, bass.ds(n * GRP, GRP)]

            def gate_rows(n, g, r, token, some):
                slots = 2 if len(some) == 4 else 4
                if not isinstance(g, int) or g >= 2:
                    pool.wait_ge(w_full, g - (slots - 1))
                    pool.nop().then_inc(pool_passed, 1)
                if not isinstance(n, int) or n:
                    pool.wait_ge(hot2_pool, n)
                    pool.nop().then_inc(pool_passed, 1)
                four = slice(token, token + 4) if isinstance(token, int) else bass.ds(token, 4)
                pool.tensor_copy(four_picks, picksT[:, 1:3, four]).then_inc(picks_copied, 1)
                pool.wait_ge(picks_copied, n + 1)
                pool.nop().then_inc(pool_passed, 1)
                for j in some:
                    ins = pool.tensor_scalar(hot2[r][:, j], lane, four_picks[:, 0, j:j + 1], four_picks[:, 1, j:j + 1],
                                             ALU.is_equal, ALU.mult)
                ins.then_inc(hot2_pool, 1)

            pool.wait_ge(pool_const, 2)
            stored(pool, ("kT", 1))
            for g in range(2):
                gate_rows(g, g, g, 4 * g, range(4))
            with pool.Fori(1, EARLY // 2) as m:
                for r in range(2):
                    gate_rows(m * 2 + r, m * 2 + r, r, m * 8 + 4 * r, range(4))
            stored(pool, ("kT", 2), ("kT", 3))
            pool.wait_ge(hot1_act, EARLY)
            with pool.Fori(EARLY // 4, DT * DS_GROUPS // 4) as m:
                for e in range(2):
                    gate_rows(m * 2 + (EARLY // 2 + e), m * 4 + (2 * e + 1), 2 * e + 1, m * 16 + (8 * e + 4),
                              range(4 - POOL_ROWS, 4))

            multiplied(pool, *group("h2T"))
            pool.wait_ge(idx_ready, 1)
            pool.wait_ge(w_stored[0], 32)
            pool.wait_ge(w_stored[1], 32)
            pool.tensor_copy(idx_u, group_of(0)).then_inc(idx_u_set, 1)
            pool.wait_ge(idx_u_set, 1)
            gather(u_exp, u_rows, idx_u, u_rows_in)
            pool.tensor_copy(idx_v, group_of(0)).then_inc(idx_v_set, 1)
            pool.wait_ge(idx_v_set, 1)
            gather(v_exp, v_rows, idx_v, v_rows_in)

            def next_rows(n):
                pool.wait_ge(u_rows_used, n + 1)
                pool.nop().then_inc(pool_passed, 1)
                pool.tensor_copy(idx_u, group_of(n + 1)).then_inc(idx_u_set, 1)
                pool.wait_ge(idx_u_set, n + 2)
                pool.nop().then_inc(pool_passed, 1)
                gather(u_exp, u_rows, idx_u, u_rows_in)
                pool.wait_ge(v_rows_used, n + 1)
                pool.nop().then_inc(pool_passed, 1)
                pool.tensor_copy(idx_v, group_of(n + 1)).then_inc(idx_v_set, 1)
                pool.wait_ge(idx_v_set, n + 2)
                pool.nop().then_inc(pool_passed, 1)
                gather(v_exp, v_rows, idx_v, v_rows_in)

            with pool.Fori(0, N_STEP - 1) as n:
                next_rows(n)
            for t in range(NT):
                norm(3, t)

        @block.tensor
        def _(pe):
            def start(*job):
                if JOBS[job] >= 8:
                    pe.wait_ge(free(*job), JOBS[job] // 8)
                return bank(*job)

            def full(last, *job):
                last.then_inc(bank_full[JOBS[job] % 8], 1)

            def arrived(*block):
                return landed(pe, *block)

            def product(job, pairs):
                o = start(*job)
                for k, (a, b) in enumerate(pairs):
                    last = pe.matmul(o[:, :], a, b, start=(k == 0), stop=(k == len(pairs) - 1))
                full(last, *job)

            def transposes(job, blocks):
                o = start(*job)
                for k, a in enumerate(blocks):
                    last = pe.transpose(o[:, k * P:(k + 1) * P], a, ident[:, :])
                full(last, *job)

            pe.wait_ge(hot_in, 16)
            pe.wait_ge(rel_in, 16)
            for f in range(2):
                o = start("ext", f)
                full(pe.matmul(o[0:H, :], rel_sb, hot_sb[:, f * HALF:(f + 1) * HALF], start=True, stop=True),
                     "ext", f)
            pe.wait_ge(cond_ready, KD)
            for b in range(ADA_FIRST):
                w = arrived("ada", b)
                product(("ada", b), [(cond[:, k, :], w[:, k, :]) for k in range(KD)])
            pe.wait_ge(ident_landed, 32)
            for t in range(NT):
                pe.wait_ge(h_ready, t + 1)
                for f in range(2):
                    transposes(("hT", t, f), [nat[:, t, (4 * f + k) * P:(4 * f + k + 1) * P] for k in range(4)])
            pe.wait_ge(bias_in, 16)
            pe.wait_ge(ident_landed, 32)
            for h in range(H):
                product(("bt", h), [(anti, flipped[:, h, :])])
            stored(pe, *group("hT"))
            def project(*jobs):
                for _, b, j in jobs:
                    w = arrived("in", b)
                    cut = slice(j * P, (j + 1) * P)
                    product(("in", b, j), [(w[:, k, cut], hT[:, k, :]) if b < 2 else (hT[:, k, cut], w[:, k, :])
                                           for k in range(KD)])

            def logits(h):
                r0 = DH * (h % 2)
                for i in range(NT):
                    o = start("s", h, i)
                    w = P * (i + 1)
                    full(pe.matmul(o[:, 0:w], qT[r0:r0 + DH, h // 2, i * P:(i + 1) * P],
                                   kT[r0:r0 + DH, h // 2, 0:w], start=True, stop=True), "s", h, i)

            for kind, b in BLOCKS[ADA_FIRST:BLOCK_NO["in", GATE_BLK]]:
                if kind == "in":
                    project(*[("in", b, j) for j in range(4)])
                else:
                    pe.wait_ge(cond_ready, KD + 1)
                    pe.wait_ge(chunks_summed, b - ADA_FIRST + 1)
                    product(("ada", b), [(cond[:, 0, :], blk(BLOCK_NO["ada", b])[:, 0, :])])
            project(*gate_jobs(0, 2))
            pe.wait_ge(ws_masked, 1)
            pe.wait_ge(v_normed, NT)
            for q in range(4):
                o = start("mix", q)
                for e in range(2):
                    g = 2 * q + e
                    last = pe.matmul(o[:, e * 256:(e + 1) * 256], wsT[:, g, :], zv[:, :, g * GD:(g + 1) * GD],
                                     start=True, stop=True)
                full(last, "mix", q)
            stored(pe, *[("in", b, j) for b in range(3) for j in range(4)])
            logits(0)
            project(*gate_jobs(2, 4))
            pe.wait_ge(yg_ready, G)
            for t in range(NT):
                transposes(("gT", t), [zu[:, t, k * P:(k + 1) * P] for k in range(4)])
            for h in range(H):
                if h + 1 < H:
                    logits(h + 1)
                project(*gates_before(h))
                for i in range(NT):
                    pe.wait_ge(p_ready, NT * h + i + 1)
                    transposes(("pT", h, i), [prob(h, i)[:, j * P:(j + 1) * P] for j in range(i + 1)])
                project(*gates_behind(h))
                stored(pe, *[("pT", h, i) for i in range(NT)])
                o = start("pv", h)
                r0 = DH * (h % 2)
                for j in range(NT):
                    last = pe.matmul(o[r0:r0 + DH, j * P:S], va[:, j, h * DH:(h + 1) * DH],
                                     pT[:, h % 2, j, j * P:S], start=(j == 0), stop=(j == NT - 1))
                full(last, "pv", h)
            stored(pe, *group("pv"), *group("gT"))
            wb = [arrived("branch", 0), arrived("branch", 1)]
            for t in range(NT):
                cut = slice(t * P, (t + 1) * P)
                for f in range(2):
                    product(("ba", t, f), [(yaT[:, k, cut], wb[f][:, k, :]) for k in range(4)])
                    product(("bg", t, f), [(ygT[:, k, cut], wb[f][:, 4 + k, :]) for k in range(4)])
            for t in range(NT):
                for f in range(2):
                    pe.wait_ge(merged, 2 * t + f + 1)
                    transposes(("mT", t, f), [ga[:, t, (4 * f + k) * P:(4 * f + k + 1) * P] for k in range(4)])
            wo = [arrived("out", 0), arrived("out", 1)]
            def mixer_out(t):
                stored(pe, ("mT", t, 0), ("mT", t, 1))
                for f in range(2):
                    product(("y", t, f), [(mT[:, k, t * P:(t + 1) * P], wo[f][:, k, :]) for k in range(KD)])

            mixer_out(0)
            mixer_out(1)
            pe.wait_ge(wq_in, 32)
            pe.wait_ge(keys_in, 16)
            for t in range(NT):
                cut = slice(t * P, (t + 1) * P)
                pe.wait_ge(h2_ready, t + 1)
                for f in range(2):
                    rows = h2_0 if t == 0 else h2[:, t]
                    transposes(("h2T", t, f), [rows[:, (4 * f + k) * P:(4 * f + k + 1) * P] for k in range(4)])
                stored(pe, ("h2T", t, 0), ("h2T", t, 1))
                for f in range(2):
                    o = start("pq", t, f)
                    for j in range(4):
                        for k in range(KD):
                            last = pe.matmul(o[:, j * P:(j + 1) * P], wq[:, f, k, j * P:(j + 1) * P], h2T[:, k, cut],
                                             start=(k == 0), stop=(k == KD - 1))
                    full(last, "pq", t, f)
                stored(pe, ("pq", t, 0), ("pq", t, 1))
                for q in range(4):
                    o = start("sc", t, q)
                    for e in range(2):
                        last = pe.matmul(o[:, e * 256:(e + 1) * 256], pqT[:, 2 * q + e, :], skb,
                                         start=True, stop=True)
                    full(last, "sc", t, q)
                if t + 2 < NT:
                    mixer_out(t + 2)

            def picks_across(t):
                pe.wait_ge(picks_ready, t + 1)
                transposes(("kT", t), [picks[t][:, a, :] for a in range(3)])

            picks_across(1)
            stored(pe, *[j for j in JOBS if JOBS[j] >= JOBS["kT", 1] - 7 and j not in (("kT", 2), ("kT", 3))])

            def spread(g, place, share):
                r = place % 2
                if share is None:
                    pe.wait_ge(hot1_act, g + 1)
                    pe.wait_ge(hot2_pool, g + 1)
                else:
                    pe.wait_ge(hots_dve, g - (EARLY - 1))
                    if r == 1:
                        pe.wait_ge(hot2_pool, share + 1)
                if isinstance(g, int):
                    if g >= 2:
                        pe.wait_ge(w_staged, g - 1)
                else:
                    pe.wait_ge(w_staged, g - 1)
                for j in range(4):
                    last = pe.matmul(banks[6 + r][:, j * P:(j + 1) * P], hot1[place][:, j], hot2[place][:, j],
                                     start=True, stop=True)
                last.then_inc(w_full, 1)

            for g in range(2):
                spread(g, g, None)
            with pe.Fori(1, EARLY // 2) as m:
                for r in range(2):
                    spread(m * 2 + r, r, None)
            pe.wait_ge(w_staged, EARLY)
            picks_across(2)
            picks_across(3)
            stored(pe, ("kT", 2), ("kT", 3))
            with pe.Fori(EARLY // 4, DT * DS_GROUPS // 4) as m:
                for q in range(4):
                    spread(m * 4 + q, q, m * 2 + (EARLY // 2 + q // 2))

            def first(j, r):
                pe.wait_ge(u_lo_done, j + 1)
                if not isinstance(j, int) or j >= 2:
                    pe.wait_ge(gel_done, j - 1)
                o = banks[6 + r][:, 0:DS]
                for k in range(KD):
                    pe.matmul(o, u_hi[:, r, k], h2_hi[:, k], start=(k == 0), stop=False)
                    pe.matmul(o, u_hi[:, r, k], h2_lo[:, k], start=False, stop=False)
                    last = pe.matmul(o, u_lo[:, r, k], h2_hi[:, k], start=False, stop=(k == KD - 1))
                last.then_inc(a_full, 1)

            def second(j, r):
                pe.wait_ge(v_lo_done, j + 1)
                pe.wait_ge(g_lo_done, j + 1)
                is_first, is_last = (isinstance(j, int) and j == n for n in (0, NK - 1))
                for t in range(DT):
                    cut = slice(t * P, (t + 1) * P)
                    for f in range(2):
                        o, half = banks[2 * t + f][:, :], slice(f * HALF, (f + 1) * HALF)
                        pe.matmul(o, g_hi[:, r, cut], v_hi[:, r, half], start=is_first, stop=False)
                        pe.matmul(o, g_hi[:, r, cut], v_lo[:, r, half], start=False, stop=False)
                        last = pe.matmul(o, g_lo[:, r, cut], v_hi[:, r, half], start=False, stop=is_last)
                last.then_inc(v_done, 1)

            pe.wait_ge(w_staged, DT * DS_GROUPS)
            pe.wait_ge(h2_lo_done, 1)
            first(0, 0)
            for q in range(STEP):
                first(q + 1, (q + 1) % 2)
                second(q, q % 2)
            with pe.Fori(1, N_STEP - 1) as n:
                for q in range(STEP):
                    first(n * STEP + (q + 1), (q + 1) % 2)
                    second(n * STEP + q, q % 2)
            for b in range(NK - STEP, NK):
                if b + 1 < NK:
                    first(b + 1, (b + 1) % 2)
                second(b, b % 2)

        @block.scalar
        def _(act):
            def quads(a, t, f):
                return a[:, 4 * f:4 * f + 4, t * P:(t + 1) * P]

            def four(o):
                return o[:, :].rearrange("p (k t) -> p k t", k=4)

            def squares(k, t, a, spare):
                if NT * k + t:
                    act.wait_ge(sq_ready, NT * k + t)
                act.activation(spare, a, ACT.Square, accum_out=sumsq(k, t)).then_inc(sq_ready, 1)

            act.wait_ge(c_in, 16)
            act.activation(ecol, ccol, ACT.Exp, scale=-1.0).then_inc(cond_exp, 1)
            for f in range(2):
                o = take(act, "ext", f)
                act.activation(ext[:, f * HALF:(f + 1) * HALF], o[0:H, :], ACT.Copy).then_inc(free("ext", f), 1)
            for t in range(NT):
                act.wait_ge(x_in[t], 16)
                squares(0, t, xr[:, t, :], junk)
            for t in range(NT):
                for f in range(2):
                    o = take(act, "hT", t, f)
                    act.activation(quads(hT, t, f), four(o), ACT.Copy).then_inc(free("hT", t, f), 1)
            for h in range(H):
                o = take(act, "bt", h)
                act.activation(bias[:, h, :], o[:, :], ACT.Copy).then_inc(free("bt", h), 1)
            act.wait_ge(sq_ready, NT)
            for b in range(GATE_BLK):
                if b == 2:
                    continue
                for j in range(4):
                    o = take(act, "in", b, j)
                    done = free("in", b, j)
                    if b == 0:
                        act.activation(qT[:, j, :], o[:, :], ACT.Copy, scale=DH ** -0.5).then_inc(done, 1)
                    elif b == 1:
                        act.activation(kT[:, j, :], o[:, :], ACT.Copy).then_inc(done, 1)
                    else:
                        act.activation((zu, zv)[b - 3][:, j, :], o[:, :], ACT.Gelu_apprx_tanh).then_inc(done, 1)

            def gates(jobs):
                for _, b, j in jobs:
                    o = take(act, "in", b, j)
                    gate, f = (ga, b - 5) if b < 7 else (gg, b - 7)
                    act.activation(gate[:, j, f * HALF:(f + 1) * HALF], o[:, :], ACT.Tanh, scale=0.5)\
                        .then_inc(free("in", b, j), 1)

            def soft(h):
                for i in range(NT):
                    act.wait_ge(max_ready, NT * h + i + 1)
                    act.activation(prob(h, i), prob(h, i), ACT.Exp, bias=nmx(h, i), accum_out=rsum(h, i))\
                        .then_inc(exp_ready, 1)

            act.wait_ge(mods_ready, 1)
            gates(gate_jobs(0, 4))
            soft(0)
            multiplied(act, *group("mix"))
            for t in range(NT):
                o = take(act, "gT", t)
                act.activation(ygT[:, :, t * P:(t + 1) * P], four(o), ACT.Copy).then_inc(free("gT", t), 1)
            for h in range(H):
                if h + 1 < H:
                    soft(h + 1)
                gates(gates_before(h))
                if h >= 2:
                    multiplied(act, ("pv", h - 2))
                for i in range(NT):
                    o = take(act, "pT", h, i)
                    w = P * (i + 1)
                    act.activation(pT[:, h % 2, 0:i + 1, i * P:(i + 1) * P],
                                   o[:, 0:w].rearrange("p (j q) -> p j q", j=i + 1), ACT.Copy)\
                        .then_inc(free("pT", h, i), 1)
                gates(gates_behind(h))
                r0 = DH * (h % 2)
                o = take(act, "pv", h)
                act.activation(yaT[r0:r0 + DH, h // 2, :], o[r0:r0 + DH, :], ACT.Copy).then_inc(free("pv", h), 1)
            for t in range(NT):
                for f in range(2):
                    if (t, f) == (0, 0):
                        multiplied(act, ("pv", H - 1))
                    o = take(act, "mT", t, f)
                    act.activation(quads(mT, t, f), four(o), ACT.Copy, scale=0.5).then_inc(free("mT", t, f), 1)
            def mixer_out(t):
                for f in range(2):
                    o = take(act, "y", t, f)
                    act.activation(nat[:, t, f * HALF:(f + 1) * HALF], o[:, :], ACT.Copy)\
                        .then_inc(free("y", t, f), 1)
                stored(act, ("y", t, 0), ("y", t, 1))

            sq = [NT]

            def squares_of(k, t, a, spare):
                act.wait_ge(sq_ready, sq[0])
                act.activation(spare, a, ACT.Square, accum_out=sumsq(k, t)).then_inc(sq_ready, 1)
                sq[0] += 1

            def gates_exp(t):
                act.wait_ge(picked, t + 1)
                if t >= 2:
                    act.wait_ge(picks_ready, t - 1)
                act.activation(expd[t % 2], shifted[:, t % 2], ACT.Exp).then_inc(expd_ready, 1)

            def x_squares(t):
                act.wait_ge(x_new, t + 1)
                squares_of(2, t, xr[:, t, :], junk2)

            act.wait_ge(p_ready, NT * H)
            multiplied(act, *group("ba"), *group("bg"))
            mixer_out(0)
            squares_of(1, 0, nat[:, 0, :], junk2)
            mixer_out(1)
            squares_of(1, 1, nat[:, 1, :], junk2)
            x_squares(0)
            x_squares(1)
            for t in range(NT):
                for f in range(2):
                    o = take(act, "h2T", t, f)
                    act.activation(quads(h2T, t, f), four(o), ACT.Copy).then_inc(free("h2T", t, f), 1)
                if t:
                    multiplied(act, *[("sc", t - 1, q) for q in range(4)])
                for f in range(2):
                    o = take(act, "pq", t, f)
                    act.activation(pqT[:, 4 * f:4 * f + 4, :], four(o), ACT.Copy).then_inc(free("pq", t, f), 1)
                if t >= 2:
                    act.wait_ge(picked, t - 1)
                else:
                    act.wait_ge(merge_read, 1)
                for q in range(4):
                    o = take(act, "sc", t, q)
                    act.activation(scores[:, t % 2, 2 * q:2 * q + 2, :], o[:, :].rearrange("p (e k) -> p e k", e=2),
                                   ACT.Copy).then_inc(free("sc", t, q), 1)
                if t + 2 < NT:
                    mixer_out(t + 2)
                    squares_of(1, t + 2, nat[:, t + 2, :], junk2)
                if t in (1, 2):
                    gates_exp(t - 1)
                if 2 <= t + 1 < NT:
                    x_squares(t + 1)

            def picks_across(t):
                o = take(act, "kT", t)
                act.activation(picksT[:, :, (t - 1) * P:t * P], o[:, 0:3 * P].rearrange("p (a t) -> p a t", a=3),
                               ACT.Copy).then_inc(free("kT", t), 1)

            def stage(g, r, t, at_token):
                act.wait_ge(w_full, g + 1)
                o = banks[6 + r][:, :].rearrange("p (t b) -> p b t", t=4)
                tokens = slice(at_token, at_token + 4) if isinstance(at_token, int) else bass.ds(at_token, 4)
                act.activation(staged[t % 2][:, :, tokens], o, ACT.Copy).then_inc(w_staged, 1)

            def stages(t, lo, hi):
                with act.Fori(lo, hi) as m:
                    for r in range(2):
                        stage(m * 2 + (t * DS_GROUPS + r), r, t, m * 8 + 4 * r)

            def first_hots(g, r, token):
                if not isinstance(g, int) or g >= 2:
                    act.wait_ge(w_full, g - 1)
                if not isinstance(g, int) or g >= 1:
                    act.wait_ge(hot1_act, g)
                for j in range(4):
                    at_t = slice(token + j, token + j + 1) if isinstance(token, int) else bass.ds(token + j, 1)
                    ins = act.activation(apart[:, j], lane, ACT.Abs, bias=picksT[:, 0, at_t], scale=-1.0)
                ins.then_inc(apart_done, 1)
                act.wait_ge(apart_done, g + 1)
                act.activation(hot1[r], apart, ACT.Relu, bias=one, scale=-1.0).then_inc(hot1_act, 1)

            def hots_and_stages(lo, hi):
                with act.Fori(lo, hi) as m:
                    for r in range(2):
                        stage(m * 2 + (r - 2), r, 0, m * 8 + (4 * r - 8))
                        first_hots(m * 2 + r, r, m * 8 + 4 * r)

            picks_across(1)
            act.wait_ge(h2_ready, NT)
            act.wait_ge(sq_ready, sq[0])
            multiplied(act, *group("y"))
            act.wait_ge(pool_const, 2)
            multiplied(act, *group("sc"))
            stored(act, ("kT", 1))
            first_hots(0, 0, 0)
            first_hots(1, 1, 4)
            hots_and_stages(1, EARLY // 4)
            gates_exp(2)
            multiplied(act, *group("h2T"))
            act.activation(h2_hi, h2T[:, :, P:S], ACT.Copy).then_inc(h2_hi_done, 1)
            hots_and_stages(EARLY // 4, EARLY // 2)
            for r in range(2):
                stage(EARLY - 2 + r, r, 0, 4 * (EARLY - 2 + r))
            gates_exp(3)
            picks_across(2)
            picks_across(3)
            stages(0, EARLY // 2, DS_GROUPS // 2)
            act.wait_ge(h2_lo_done, 1)
            multiplied(act, ("kT", 2), *group("pq"))
            stages(1, 0, DS_GROUPS // 2)
            act.wait_ge(w_stored[0], 16)
            stages(2, 0, DS_GROUPS // 2)

            def u_high(j, q):
                r = q % 2
                act.wait_ge(u_raw_in[q], 16 * turn(j, q))
                if not isinstance(j, int) or j >= 2:
                    act.wait_ge(a_full, j - 1)
                act.activation(u_hi[:, r], u_raw[:, q], ACT.Copy).then_inc(u_hi_done, 1)

            def v_high(j, q):
                r = q % 2
                act.wait_ge(v_raw_in[q], 16 * turn(j, q))
                if not isinstance(j, int) or j >= 2:
                    act.wait_ge(v_done, j - 1)
                act.activation(v_hi[:, r], v_raw[:, q], ACT.Copy).then_inc(v_hi_done, 1)

            def block_step(b, q):
                r = q % 2
                act.wait_ge(a_full, b + 1)
                if not isinstance(b, int) or b >= 2:
                    act.wait_ge(gated_done, b - 1)
                act.activation(gel[:, r], banks[6 + r][:, 0:DS], ACT.Gelu_apprx_tanh).then_inc(gel_done, 1)
                if not isinstance(b, int) or b + 2 < NK:
                    u_high(b + 2, (q + 2) % STEP)
                act.wait_ge(gated_done, b + 1)
                if not isinstance(b, int) or b >= 2:
                    act.wait_ge(v_done, b - 1)
                act.activation(g_hi[:, r], gated[:, r], ACT.Copy).then_inc(g_hi_done, 1)
                if not isinstance(b, int) or b + 1 < NK:
                    v_high(b + 1, (q + 1) % STEP)

            def own_gelu(n):
                act.wait_ge(u_rows_used, n + 1)
                act.activation(dots_gelu, dots, ACT.Gelu_apprx_tanh).then_inc(own_gelu_done, 1)

            u_high(0, 0)
            u_high(1, 1)
            v_high(0, 0)
            for q in range(STEP):
                block_step(q, q)
            own_gelu(0)
            with act.Fori(1, N_STEP - 1) as n:
                for q in range(STEP):
                    block_step(n * STEP + q, q)
                    if q == 1:
                        own_gelu(n)
            for q in range(STEP):
                block_step(NK - STEP + q, q)
                if q == 1:
                    own_gelu(N_STEP - 1)
            act.wait_ge(v_done, NK)
            for t in range(DT):
                for f in range(2):
                    act.activation(y_out[:, t, f * HALF:(f + 1) * HALF], banks[2 * t + f][:, :], ACT.Copy)\
                        .then_inc(y_taken, 1)
            act.wait_ge(v_rows_used, N_STEP)
            squares_of(3, 0, acc0, junk3)
            for t in range(1, NT):
                act.wait_ge(y_taken, 2 * t)
                squares_of(3, t, y_out[:, t - 1], junk3)

        @block.vector
        def _(dve):
            chain = [0]

            def link(ins):
                chain[0] += 1
                ins.then_inc(dve_chain, 1)
                dve.wait_ge(dve_chain, chain[0])

            dve.wait_ge(cond_exp, 1)
            link(dve.tensor_scalar(scol, ecol, 1.0, None, ALU.add))
            link(dve.reciprocal(scol, scol))
            link(dve.tensor_tensor(scol, scol, ccol, ALU.mult))
            for k in range(KD):
                dve.tensor_copy(cond[:, k, :], scol[:, k:k + 1].to_broadcast([P, P])).then_inc(cond_ready, 1)
            dve.wait_ge(ada_b_in, 32)

            def plus_bias(b):
                o = take(dve, "ada", b)
                half = mod(b // 2)[:, (b % 2) * HALF:(b % 2 + 1) * HALF]
                dve.tensor_tensor(half, o[:, :], half, ALU.add).then_inc(free("ada", b), 1)

            def with_gain(row, gain, one):
                link(dve.scalar_tensor_tensor(mod(row), mod(row), one, gains[:, gain, :], ALU.add, ALU.mult))

            for b in range(ADA_FIRST):
                plus_bias(b)
            dve.memset(cond[:, 0, :], 1.0).then_inc(cond_ready, 1)
            dve.wait_ge(gains_in, 16)
            stored(dve, *[("ada", b) for b in range(ADA_FIRST)])
            with_gain(1, 0, 1.0)
            for t in range(NT):
                dve.wait_ge(rstd_ready, t + 1)
                link(dve.scalar_tensor_tensor(nat[:, t, :], xr[:, t, :], rstd(0, t), mod(1),
                                              ALU.mult, ALU.mult))
                dve.tensor_tensor(nat[:, t, :], nat[:, t, :], mod(0), ALU.add).then_inc(h_ready, 1)
            for kind, b in BLOCKS[ADA_FIRST:BLOCK_NO["in", GATE_BLK]]:
                if kind == "ada":
                    w = landed(dve, "ada", b)
                    ins = dve.tensor_scalar(w[:, 0, :], w[:, 0, :], scol[:, 0:1], None, ALU.mult)
                    for k in range(1, KD):
                        link(ins)
                        ins = dve.scalar_tensor_tensor(w[:, 0, :], w[:, k, :], scol[:, k:k + 1], w[:, 0, :],
                                                       ALU.mult, ALU.add)
                    ins.then_inc(chunks_summed, 1)
                    plus_bias(b)
                elif b == 2:
                    for t in range(NT):
                        o = take(dve, "in", 2, t)
                        dve.tensor_copy(va[:, t, :], o[:, :]).then_inc(free("in", 2, t), 1)
            stored(dve, *group("ada"))
            for row, gain, one in ((2, 1, 0.0), (4, 2, 1.0), (5, 3, 0.0)):
                with_gain(row, gain, one)
            dve.nop().then_inc(mods_ready, 1)
            for t in range(NT):
                stored(dve, ("in", 4, t))
                link(dve.bn_stats(bn(t), zv[:, t, :]))
                dve.bn_aggr(mv(t), bn(t)).then_inc(v_var, 1)
            dve.wait_ge(ln_in, 16)
            dve.wait_ge(v_var, NT)
            for t in range(NT):
                dve.wait_ge(v_rs, t + 1)
                link(dve.tensor_scalar(zv[:, t, :], zv[:, t, :], mv(t)[:, 0:1], v_rstd(t), ALU.subtract, ALU.mult))
                link(dve.tensor_tensor(zv[:, t, :], zv[:, t, :], ln_row[:, 0, :], ALU.mult))
                dve.tensor_tensor(zv[:, t, :], zv[:, t, :], ln_row[:, 1, :], ALU.add).then_inc(v_normed, 1)
            dve.wait_ge(v_normed, NT)
            dve.wait_ge(bs_in, 16)
            stored(dve, *[("in", 3, t) for t in range(NT)])
            for q in range(4):
                o = take(dve, "mix", q)
                for e in range(2):
                    g = 2 * q + e
                    u = zu[:, :, g * GD:(g + 1) * GD]
                    ins = dve.scalar_tensor_tensor(u, o[:, e * 256:(e + 1) * 256].rearrange("p (n c) -> p n c", n=NT),
                                                   bs[:, g:g + 1], u, ALU.add, ALU.mult)
                    ins.then_inc(yg_ready, 1)
                dve.wait_ge(yg_ready, 2 * q + 2)
                dve.nop().then_inc(free("mix", q), 1)

            def biased(h):
                if h >= 2:
                    multiplied(dve, *[("pT", h - 2, i) for i in range(NT)])
                for i in range(NT):
                    o = take(dve, "s", h, i)
                    w = P * (i + 1)
                    link(dve.tensor_tensor_reduce(out=prob(h, i), in0=o[:, 0:w], in1=bias[:, h, S - w:S], scale=1.0,
                                                  scalar=LOWEST, op0=ALU.add, op1=ALU.max, accum_out=mx(h, i)))
                    dve.nop().then_inc(free("s", h, i), 1)
                    dve.tensor_scalar(nmx(h, i), mx(h, i), -1.0, None, ALU.mult).then_inc(max_ready, 1)

            def normed(h):
                for i in range(NT):
                    dve.wait_ge(exp_ready, NT * h + i + 1)
                    link(dve.reciprocal(rinv(h, i), rsum(h, i)))
                    dve.tensor_scalar(prob(h, i), prob(h, i), rinv(h, i), None, ALU.mult).then_inc(p_ready, 1)

            stored(dve, *group("bt"))
            biased(0)
            for h in range(H):
                if h + 1 < H:
                    biased(h + 1)
                normed(h)
            stored(dve, *group("in"))
            for t in range(NT):
                for f in range(2):
                    cut = slice(f * HALF, (f + 1) * HALF)
                    o = take(dve, "ba", t, f)
                    dve.scalar_tensor_tensor(ga[:, t, cut], ga[:, t, cut], 1.0, o[:, :], ALU.add, ALU.mult)\
                        .then_inc(free("ba", t, f), 1)
                    o = take(dve, "bg", t, f)
                    dve.scalar_tensor_tensor(gg[:, t, cut], gg[:, t, cut], 1.0, o[:, :], ALU.add, ALU.mult)\
                        .then_inc(free("bg", t, f), 1)
                    stored(dve, ("ba", t, f), ("bg", t, f))
                    dve.tensor_tensor(ga[:, t, cut], ga[:, t, cut], gg[:, t, cut], ALU.add).then_inc(merged, 1)
            dve.nop().then_inc(merge_read, 1)

            def x_step(t):
                dve.wait_ge(rstd_ready, NORM_NO[1, t])
                dve.wait_ge(x_in[t], 32)
                link(dve.scalar_tensor_tensor(nat[:, t, :], nat[:, t, :], rstd(1, t), mod(2), ALU.mult, ALU.mult))
                dve.tensor_tensor(xr[:, t, :], xr[:, t, :], nat[:, t, :], ALU.add).then_inc(x_new, 1)

            def h2_step(t):
                rows = h2_0 if t == 0 else h2[:, t]
                dve.wait_ge(rstd_ready, NORM_NO[2, t])
                link(dve.scalar_tensor_tensor(rows, xr[:, t, :], rstd(2, t), mod(4), ALU.mult, ALU.mult))
                dve.tensor_tensor(rows, rows, mod(3), ALU.add).then_inc(h2_ready, 1)

            base, ticks = [0], [0]

            def tick(ins):
                ticks[0] += 1
                ins.then_inc(dve_tick, 1)
                return ticks[0]

            waited = [0]

            def after(n):
                if n > waited[0]:
                    waited[0] = n
                    dve.wait_ge(dve_tick, base[0] + n)

            def after_apart(n):
                if n > waited[0]:
                    after(n)
                    dve.nop().then_inc(dve_passed, 1)

            def pair(step):
                return [step(e) for e in range(2)]

            def top_two_sides(t, two):
                def places(e):
                    return bass.ds(two * (2 * TOPK) + e * TOPK, TOPK)

                def scores_of(e):
                    source = scores[:, t % 2, bass.ds(two * 2 + e, 1), :].rearrange("p o (a k) -> p (o a) k", a=2)
                    return tick(dve.tensor_copy(cur[e], source))

                def best_eight(e, lo, n):
                    after_apart(n)
                    return [tick(dve.max(top[e][:, a, lo:lo + 8], cur[e][:, a, :])) for a in range(2)][-1]

                def without_them(e, n):
                    after_apart(n)
                    for a in range(2):
                        dve.max_index(top_i[e][:, a, 0:8], top[e][:, a, 0:8], cur[e][:, a, :])
                    return [tick(dve.match_replace(cur[e][:, a, :], top[e][:, a, 0:8], cur[e][:, a, :], LOWEST))
                            for a in range(2)][-1]

                m = pair(scores_of)
                m = pair(lambda e: best_eight(e, 0, m[e]))
                m = pair(lambda e: without_them(e, m[e]))
                m = pair(lambda e: best_eight(e, 8, m[e]))

                def sums(e):
                    after_apart(m[e])
                    for a in range(2):
                        dve.max_index(top_i[e][:, a, 8:16], top[e][:, a, 8:16], cur[e][:, a, :])
                    for (i0, i1, nj) in ((0, CORNER, TOPK), (CORNER, TOPK, CORNER)):
                        lo, n = (0, CORNER * TOPK) if i0 == 0 else (CORNER * TOPK, CANDS - CORNER * TOPK)
                        shape = [P, i1 - i0, nj]
                        last = tick(dve.tensor_tensor(
                            cand[e][:, lo:lo + n].rearrange("p (i j) -> p i j", j=nj),
                            top[e][:, 0, i0:i1].unsqueeze(2).to_broadcast(shape),
                            top[e][:, 1, 0:nj].unsqueeze(1).to_broadcast(shape), ALU.add))
                    return last

                def best_sums(e, lo):
                    after_apart(m[e])
                    return tick(dve.max(best[e][:, lo:lo + 8], cand[e]))

                def sums_without(e):
                    after_apart(m[e])
                    dve.max_index(place_i[e][:, 0:8], best[e][:, 0:8], cand[e])
                    return tick(dve.match_replace(cand[e], best[e][:, 0:8], cand[e], LOWEST))

                def last_places(e):
                    after_apart(m[e])
                    tick(dve.tensor_copy(top_f[e], top_i[e]))
                    return tick(dve.max_index(place_i[e][:, 8:16], best[e][:, 8:16], cand[e]))

                m = pair(sums)
                m = pair(lambda e: best_sums(e, 0))
                m = pair(sums_without)
                m = pair(lambda e: best_sums(e, 8))
                m = pair(last_places)

                def shifts(e):
                    after(m[e])
                    dve.tensor_scalar(shifted[:, t % 2, places(e)], best[e], best[e][:, 0:1], None, ALU.subtract)
                    for n, by in ((1, 4), (2, 2)):
                        last = tick(dve.tensor_single_scalar(place_i[e][:, n * TOPK:(n + 1) * TOPK],
                                                             place_i[e][:, 0:TOPK], by, ALU.logical_shift_right))
                    return last

                def as_numbers(e):
                    after(m[e])
                    return tick(dve.tensor_copy(place_f[e], place_i[e]))

                m = pair(shifts)
                m = pair(as_numbers)

                def i_of(e):
                    after(m[e])
                    return tick(dve.scalar_tensor_tensor(pair_f[e][:, 0:TOPK], place_f[e][:, 2 * TOPK:3 * TOPK],
                                                         -float(TOPK - CORNER), place_f[e][:, TOPK:2 * TOPK],
                                                         ALU.add, ALU.max))

                def line(e):
                    after(m[e])
                    return tick(dve.tensor_scalar(corner[e], pair_f[e][:, 0:TOPK], float(CORNER),
                                                  float(CORNER * (TOPK - CORNER)), ALU.mult, ALU.add))

                def row_start(e):
                    after(m[e])
                    return tick(dve.scalar_tensor_tensor(corner[e], pair_f[e][:, 0:TOPK], float(TOPK), corner[e],
                                                         ALU.mult, ALU.min))

                def j_of(e):
                    after(m[e])
                    return tick(dve.tensor_tensor(pair_f[e][:, TOPK:2 * TOPK], place_f[e][:, 0:TOPK], corner[e],
                                                  ALU.subtract))

                def matches(e):
                    after(m[e])
                    return tick(dve.tensor_tensor(match[e], iota_f.unsqueeze(1).to_broadcast([P, 2 * TOPK, TOPK]),
                                                  pair_f[e].unsqueeze(2).to_broadcast([P, 2 * TOPK, TOPK]),
                                                  ALU.is_equal))

                def four_d(e):
                    return match[e].rearrange("p (a s) j -> p a s j", a=2)

                def looked_up(e):
                    after(m[e])
                    return [tick(dve.tensor_tensor(four_d(e)[:, a], four_d(e)[:, a],
                                                   top_f[e][:, a, :].unsqueeze(1).to_broadcast([P, TOPK, TOPK]),
                                                   ALU.mult)) for a in range(2)][-1]

                def keys_of(e):
                    after(m[e])
                    return tick(dve.tensor_reduce(picks[t][:, 0:2, places(e)], four_d(e), AX, ALU.add))

                for step in (i_of, line, row_start, j_of, matches, looked_up, keys_of):
                    m = pair(step)

            def pick(t):
                stored(dve, *[("sc", t, q) for q in range(4)])
                start = base[0] + ticks[0]
                with dve.Fori(0, PH // 2) as two:
                    base[0], ticks[0], waited[0] = two * HEADS_TICKS + start, 0, -1
                    after_apart(0)
                    top_two_sides(t, two)
                    assert ticks[0] == HEADS_TICKS, ticks[0]
                base[0], ticks[0], waited[0] = start + PH // 2 * HEADS_TICKS, 0, -1
                after(0)
                dve.nop().then_inc(picked, 1)

            def divide(t):
                dve.wait_ge(expd_ready, t + 1)
                heads = expd[t % 2].rearrange("p (h k) -> p h k", h=PH)
                waited[0] = -1
                after(tick(dve.tensor_reduce(esum, heads, AX, ALU.add)))
                after(tick(dve.reciprocal(einv, esum)))
                dve.tensor_tensor(picks[t][:, 2, :].rearrange("p (h k) -> p h k", h=PH), heads,
                                  einv.unsqueeze(2).to_broadcast([P, PH, TOPK]), ALU.mult).then_inc(picks_ready, 1)

            x_step(0)
            x_step(1)
            h2_step(0)
            h2_step(1)
            multiplied(dve, *group("mT"))
            dve.wait_ge(h2_ready, 2)
            tick(dve.tensor_copy(iota_f, iota_i))
            pick(0)
            divide(0)
            for t in range(2, NT):
                x_step(t)
                h2_step(t)
                pick(t - 1)
                if t == 2:
                    divide(1)
            pick(NT - 1)
            divide(2)
            dve.wait_ge(h2_hi_done, 1)
            dve.tensor_tensor(h2_lo, h2T[:, :, P:S], h2_hi.bitcast(F32), ALU.subtract).then_inc(h2_lo_done, 1)
            divide(3)
            link(dve.memset(acc0, 0.0))
            dve.wait_ge(picks_ready, NT)
            dve.scalar_tensor_tensor(idx0, picks[0][:, 0, :], float(NK), picks[0][:, 1, :], ALU.mult, ALU.add)\
                .then_inc(idx_ready, 1)

            stored(dve, ("kT", 2), ("kT", 3))
            dve.wait_ge(pool_const, 2)
            with dve.Fori(EARLY // 4, DT * DS_GROUPS // 4) as m:
                for r in range(4):
                    dve.wait_ge(w_full, m * 4 + (r - 3))
                    dve.tensor_tensor(hot1[r], lane.unsqueeze(1).to_broadcast([P, 4, P]),
                                      picksT[:, 0, bass.ds(m * 16 + 4 * r, 4)].unsqueeze(2).to_broadcast([P, 4, P]),
                                      ALU.is_equal)
                    for j in range(4 if r % 2 == 0 else 4 - POOL_ROWS):
                        token = bass.ds(m * 16 + (4 * r + j), 1)
                        ins = dve.tensor_scalar(hot2[r][:, j], lane, picksT[:, 1, token], picksT[:, 2, token],
                                                ALU.is_equal, ALU.mult)
                    ins.then_inc(hots_dve, 1)

            def u_low(j, q):
                r = q % 2
                dve.wait_ge(u_hi_done, j + 1)
                dve.tensor_tensor(u_lo[:, r], u_raw[:, q], u_hi[:, r].bitcast(F32), ALU.subtract)\
                    .then_inc(u_lo_done, 1)

            def v_low(j, q):
                r = q % 2
                dve.wait_ge(v_hi_done, j + 1)
                dve.tensor_tensor(v_lo[:, r], v_raw[:, q], v_hi[:, r].bitcast(F32), ALU.subtract)\
                    .then_inc(v_lo_done, 1)

            def block_step(b, q):
                r = q % 2
                dve.wait_ge(gel_done, b + 1)
                dve.wait_ge(w_row_in[q], 16 * turn(b, q))
                dve.tensor_tensor(gated[:, r], gel[:, r], w_row[:, q], ALU.mult).then_inc(gated_done, 1)
                if not isinstance(b, int) or b + 2 < NK:
                    u_low(b + 2, (q + 2) % STEP)
                dve.wait_ge(g_hi_done, b + 1)
                dve.tensor_tensor(g_lo[:, r], gated[:, r], g_hi[:, r].bitcast(F32), ALU.subtract)\
                    .then_inc(g_lo_done, 1)
                if not isinstance(b, int) or b + 1 < NK:
                    v_low(b + 1, (q + 1) % STEP)

            def own(n, q):
                if q == 0:
                    dve.wait_ge(u_rows_in, n * (16 * GRP) + 16 * GRP)
                if q < 2:
                    for s in (2 * q, 2 * q + 1):
                        ins = dve.scalar_tensor_tensor(u_rows[:, s], u_rows[:, s], 1.0, h2_0, ALU.mult, ALU.mult,
                                                       accum_out=dots[:, s:s + 1])
                    if q == 1:
                        ins.then_inc(u_rows_used, 1)
                    return
                if q == 2:
                    dve.wait_ge(own_gelu_done, n + 1)
                    dve.wait_ge(v_rows_in, n * (16 * GRP) + 16 * GRP)
                    gates = gate0[:, n * GRP:(n + 1) * GRP] if isinstance(n, int) else gate0[:, bass.ds(n * GRP, GRP)]
                    dve.tensor_tensor(coef, dots_gelu, gates, ALU.mult).then_inc(coef_tick, 1)
                    dve.wait_ge(coef_tick, n + 1)
                for s in (2 * q - 4, 2 * q - 3):
                    ins = dve.scalar_tensor_tensor(acc0, v_rows[:, s], coef[:, s:s + 1], acc0, ALU.mult, ALU.add)
                    if s < GRP - 1:
                        ins.then_inc(acc_tick, 1)
                        dve.wait_ge(acc_tick, n * (GRP - 1) + (s + 1))
                    else:
                        ins.then_inc(v_rows_used, 1)
                        dve.wait_ge(v_rows_used, n + 1)

            u_low(0, 0)
            u_low(1, 1)
            v_low(0, 0)
            for q in range(STEP):
                block_step(q, q)
            for q in range(STEP):
                own(0, q)
            with dve.Fori(1, N_STEP - 1) as n:
                for q in range(STEP):
                    block_step(n * STEP + q, q)
                    own(n, q)
            for q in range(STEP):
                block_step(NK - STEP + q, q)
                own(N_STEP - 1, q)
            for t in range(NT):
                rows = acc0 if t == 0 else y_out[:, t - 1]
                dve.wait_ge(rstd_ready, NORM_NO[3, t])
                link(dve.scalar_tensor_tensor(rows, rows, rstd(3, t), gate2, ALU.mult, ALU.mult))
                dve.tensor_tensor(rows, xr[:, t, :], rows, ALU.add).then_inc(out_ready, 1)


def kernel(x, c, ada_w, ada_b, pre_g1, post_g1, w_in, gmlp_ln_g, gmlp_ln_b, gmlp_w_s, gmlp_b_s, rel_bias,
           w_branch_attn, w_branch_gmlp, w_out, pre_g2, post_g2, peer_w_query, peer_sub_keys, peer_u, peer_v):
    import concourse.bacc as bacc
    from concourse.bass_utils import run_bass_kernel_spmd

    a = np.asarray
    half = QD // 2
    keys = np.zeros((QD, 2 * NK), np.float32)
    for side in range(2):
        keys[side * half:(side + 1) * half, side * NK:(side + 1) * NK] = a(peer_sub_keys)[0, side].T
    arrays = {
        "x": a(x), "c": a(c)[0].reshape(KD, P).T, "ada_w": a(ada_w)[0], "ada_b": a(ada_b)[0],
        "rows_g": np.concatenate([a(pre_g1)[0], a(post_g1)[0], a(pre_g2)[0], a(post_g2)[0]]),
        "w_in": a(w_in)[0], "ln_gb": np.stack([a(gmlp_ln_g)[0], a(gmlp_ln_b)[0]]),
        "w_s": a(gmlp_w_s)[0].transpose(2, 0, 1), "b_s": a(gmlp_b_s)[0].T, "rel": a(rel_bias),
        "w_branch": np.concatenate([a(w_branch_attn)[0], a(w_branch_gmlp)[0]]), "w_out": a(w_out)[0],
        "w_query": a(peer_w_query)[0], "keys": keys, "u_exp": a(peer_u)[0],
        "u_by_key": a(peer_u)[0].reshape(NK, NK, KD, P).transpose(1, 3, 2, 0).reshape(NK, P, KD * NK),
        "v_exp": a(peer_v)[0],
        "hot": bucket_onehot(), "ident_in": np.eye(P, dtype=np.float32),
        "anti_in": np.eye(P, dtype=np.float32)[::-1],
    }
    arrays = {k: np.ascontiguousarray(v) for k, v in arrays.items()}
    nc = bacc.Bacc("TRN2", target_bir_lowering=False, num_devices=1)
    args = [nc.dram_tensor(k, list(v.shape), F32, kind="ExternalInput").ap() for k, v in arrays.items()]
    out = nc.dram_tensor("out", [1, S, D], F32, kind="ExternalOutput").ap()
    build(nc, *args, out)
    return run_bass_kernel_spmd(nc, [arrays], core_ids=[0]).results[0]["out"]
```
